# Optimizing a Trainium2 kernel written in Bass

```python
import math
import jax, jax.numpy as jnp
from jax import lax
import numpy as np

D_MODEL = 1024
BATCH = 1
SEQ = 256
DEPTH = 2

GRID_W = 64
CTX_LEN = 256
N_MIXERS = 4
Q_BLOCK = 128
ROPE_BASE = 10000.0
EPS = 1e-6
ADA_CHUNKS = 6

RET_HEADS = 4
RET_DK = D_MODEL // RET_HEADS
RET_DV = 2 * RET_DK
RET_CHUNK = 128

DIFF_HEADS = 8
DIFF_DH = D_MODEL // (2 * DIFF_HEADS)
DIFF_DV = 2 * DIFF_DH

NA_HEADS = 16
NA_DH = D_MODEL // NA_HEADS
NA_WIN_H = 8
NA_WIN_W = 16

MLA_HEADS = 16
MLA_Q_RANK = 256
MLA_KV_RANK = 128
MLA_NOPE = 64
MLA_ROPE = 32
MLA_V = 64
MLA_QK = MLA_NOPE + MLA_ROPE

FFN_HIDDEN = -(-8 * D_MODEL // (3 * 256)) * 256


def rms_norm(x):
    xf = x.astype(jnp.float32)
    return (xf * lax.rsqrt(jnp.mean(xf * xf, axis=-1, keepdims=True) + EPS)).astype(x.dtype)

def rms_norm_gain(x, g):
    return rms_norm(x) * g.astype(x.dtype)

def modulate(x, shift, scale):
    return rms_norm(x) * (1.0 + scale) + shift

def swiglu(h, w_in, w_out):
    a, g = jnp.split(h @ w_in, 2, axis=-1)
    return (jax.nn.silu(a) * g) @ w_out

def rope_2d(x):
    n, d = x.shape[1], x.shape[-1]
    half = d // 2
    quarter = half // 2
    pos = jnp.arange(n)
    row = (pos // GRID_W).astype(jnp.float32)
    col = (pos % GRID_W).astype(jnp.float32)
    inv_freq = jnp.power(ROPE_BASE, -jnp.arange(quarter, dtype=jnp.float32) / quarter)
    bshape = (n,) + (1,) * (x.ndim - 3) + (quarter,)

    def rot(t, p):
        ang = (p[:, None] * inv_freq[None, :]).reshape(bshape)
        cos, sin = jnp.cos(ang).astype(t.dtype), jnp.sin(ang).astype(t.dtype)
        t1, t2 = t[..., :quarter], t[..., quarter:]
        return jnp.concatenate([t1 * cos - t2 * sin, t2 * cos + t1 * sin], axis=-1)

    return jnp.concatenate([rot(x[..., :half], row), rot(x[..., half:], col)], axis=-1)

def map_query_blocks(fn, q):
    b, n = q.shape[0], q.shape[1]
    qb = jnp.moveaxis(q.reshape((b, n // Q_BLOCK, Q_BLOCK) + q.shape[2:]), 1, 0)
    out = jnp.moveaxis(lax.map(fn, qb), 0, 1)
    return out.reshape((b, n) + out.shape[3:])

def softmax_attend(q, k, v, scale):
    s = jnp.einsum('bqhd,bkhd->bhqk', q, k).astype(jnp.float32) * scale
    p = jax.nn.softmax(s, axis=-1).astype(v.dtype)
    return jnp.einsum('bhqk,bkhv->bqhv', p, v)

def chunk_retention(q, k, v, log_gamma, s0):
    b, n, h, _ = q.shape
    dv = v.shape[-1]
    nc = n // RET_CHUNK
    f32 = jnp.float32

    def chunks(t):
        return jnp.moveaxis(t.astype(f32).reshape(b, nc, RET_CHUNK, h, t.shape[-1]), 1, 0)

    idx = jnp.arange(RET_CHUNK, dtype=f32)
    rel = idx[:, None] - idx[None, :]
    d_intra = jnp.where(rel >= 0, jnp.exp(jnp.maximum(rel, 0.0) * log_gamma[:, None, None]), 0.0)
    d_cross = jnp.exp((idx + 1.0)[None, :] * log_gamma[:, None]).T[None, :, :, None]
    d_state = jnp.exp((RET_CHUNK - 1.0 - idx)[None, :] * log_gamma[:, None]).T[None, :, :, None]
    d_chunk = jnp.exp(RET_CHUNK * log_gamma)[None, :, None, None]

    def step(s, qkv):
        qc, kc, vc = qkv
        att = jnp.einsum('bihd,bjhd->bhij', qc, kc) * d_intra
        o = jnp.einsum('bhij,bjhv->bihv', att, vc) + jnp.einsum('bihd,bhdv->bihv', qc, s) * d_cross
        s = s * d_chunk + jnp.einsum('bjhd,bjhv->bhdv', kc * d_state, vc)
        return s, o

    _, o = lax.scan(step, s0.astype(f32), (chunks(q), chunks(k), chunks(v)))
    return jnp.moveaxis(o, 0, 1).reshape(b, n, h, dv)

def retention_output(o, g, norm_g, w_out):
    b, n, h, dv = o.shape
    of = o.astype(jnp.float32)
    mu = jnp.mean(of, axis=-1, keepdims=True)
    var = jnp.mean(jnp.square(of - mu), axis=-1, keepdims=True)
    on = ((of - mu) * lax.rsqrt(var + EPS)).astype(g.dtype).reshape(b, n, h * dv) * norm_g
    return (on * jax.nn.silu(g)) @ w_out

def retention_mixer(h_ctx, h_lat, w_in, decay_logit, norm_g, w_out, need_ctx):
    f32 = jnp.float32
    nqk = RET_HEADS * RET_DK
    splits = [nqk, 2 * nqk, 2 * nqk + RET_HEADS * RET_DV]

    def proj(h):
        b, n, _ = h.shape
        q, k, v, g = jnp.split(h @ w_in, splits, axis=-1)
        return (q.reshape(b, n, RET_HEADS, RET_DK),
                k.reshape(b, n, RET_HEADS, RET_DK) * (RET_DK ** -0.5),
                v.reshape(b, n, RET_HEADS, RET_DV), g)

    qc, kc, vc, gc = proj(h_ctx)
    ql, kl, vl, gl = proj(h_lat)
    ql, kl = rope_2d(ql), rope_2d(kl)
    log_gamma = jax.nn.log_sigmoid(decay_logit.astype(f32))
    lf, lb = log_gamma[0], log_gamma[1]
    n_ctx = h_ctx.shape[1]
    pos = jnp.arange(n_ctx, dtype=f32)
    kcf, vcf = kc.astype(f32), vc.astype(f32)
    w_f = jnp.exp((n_ctx - 1.0 - pos)[:, None] * lf[None, :])[None, :, :, None]
    w_b = jnp.exp(pos[:, None] * lb[None, :])[None, :, :, None]
    s_f = jnp.einsum('blhk,blhv->bhkv', kcf * w_f, vcf)
    s_b = jnp.einsum('blhk,blhv->bhkv', kcf * w_b, vcf)
    o_lat = (chunk_retention(ql, kl, vl, lf, s_f)
             + chunk_retention(ql[:, ::-1], kl[:, ::-1], vl[:, ::-1], lb, s_b)[:, ::-1])
    y_lat = retention_output(o_lat, gl, norm_g, w_out)
    if not need_ctx:
        return None, y_lat
    rel = pos[:, None] - pos[None, :]
    d_bi = (jnp.where(rel >= 0, jnp.exp(jnp.maximum(rel, 0.0) * lf[:, None, None]), 0.0)
            + jnp.where(rel <= 0, jnp.exp(jnp.maximum(-rel, 0.0) * lb[:, None, None]), 0.0))
    att = jnp.einsum('bihd,bjhd->bhij', qc.astype(f32), kcf) * d_bi
    o_ctx = jnp.einsum('bhij,bjhv->bihv', att, vcf)
    return retention_output(o_ctx, gc, norm_g, w_out), y_lat

def diff_attend(q, k, v, lam, scale):
    s = jnp.einsum('bqhmd,bkhmd->bhmqk', q, k).astype(jnp.float32) * scale
    p = jax.nn.softmax(s, axis=-1)
    p = p[:, :, 0] - lam * p[:, :, 1]
    return jnp.einsum('bhqk,bkhv->bqhv', p.astype(v.dtype), v)

def diff_attention_mixer(h_ctx, h_lat, w_in, q_norm_g, k_norm_g, lam_vecs, subln_g, w_out,
                         lambda_init, need_ctx):
    nq = DIFF_HEADS * 2 * DIFF_DH

    def proj(h):
        b, n, _ = h.shape
        q, k, v = jnp.split(h @ w_in, [nq, 2 * nq], axis=-1)
        q = rms_norm_gain(q.reshape(b, n, DIFF_HEADS, 2, DIFF_DH), q_norm_g)
        k = rms_norm_gain(k.reshape(b, n, DIFF_HEADS, 2, DIFF_DH), k_norm_g)
        return q, k, v.reshape(b, n, DIFF_HEADS, DIFF_DV)

    qc, kc, vc = proj(h_ctx)
    ql, kl, vl = proj(h_lat)
    ql, kl = rope_2d(ql), rope_2d(kl)
    lv = lam_vecs.astype(jnp.float32)
    lam = jnp.exp(jnp.sum(lv[0] * lv[1])) - jnp.exp(jnp.sum(lv[2] * lv[3])) + lambda_init
    scale = DIFF_DH ** -0.5

    def out(o):
        b, n = o.shape[0], o.shape[1]
        o = rms_norm_gain(o, subln_g) * (1.0 - lambda_init)
        return o.reshape(b, n, DIFF_HEADS * DIFF_DV) @ w_out

    k_all = jnp.concatenate([kc, kl], axis=1)
    v_all = jnp.concatenate([vc, vl], axis=1)
    y_lat = out(map_query_blocks(lambda qb: diff_attend(qb, k_all, v_all, lam, scale), ql))
    if not need_ctx:
        return None, y_lat
    return out(diff_attend(qc, kc, vc, lam, scale)), y_lat

def neighborhood_mixer(h_ctx, h_lat, w_in, q_norm_g, k_norm_g, rel_bias, w_out, need_ctx):
    def proj(h):
        b, n, _ = h.shape
        q, k, v = jnp.split(h @ w_in, 3, axis=-1)
        q = rms_norm_gain(q.reshape(b, n, NA_HEADS, NA_DH), q_norm_g)
        k = rms_norm_gain(k.reshape(b, n, NA_HEADS, NA_DH), k_norm_g)
        return q, k, v.reshape(b, n, NA_HEADS, NA_DH)

    qc, kc, vc = proj(h_ctx)
    ql, kl, vl = proj(h_lat)
    scale = NA_DH ** -0.5
    b, n = ql.shape[0], ql.shape[1]
    rows = n // GRID_W
    wh = min(NA_WIN_H, rows)
    n_loc = wh * NA_WIN_W

    def grid(t):
        return t.reshape(b, rows, GRID_W, NA_HEADS, NA_DH)

    kg, vg = grid(kl), grid(vl)
    col = np.arange(GRID_W)
    col_start = np.clip(col - NA_WIN_W // 2, 0, GRID_W - NA_WIN_W)
    col_idx = col_start[:, None] + np.arange(NA_WIN_W)[None, :]
    dc_idx = col_idx - col[:, None] + (NA_WIN_W - 1)

    def row_block(args):
        r, q_row = args
        r0 = jnp.clip(r - NA_WIN_H // 2, 0, rows - wh)
        k_win = lax.dynamic_slice_in_dim(kg, r0, wh, axis=1)[:, :, col_idx]
        v_win = lax.dynamic_slice_in_dim(vg, r0, wh, axis=1)[:, :, col_idx]
        dr_idx = r0 + jnp.arange(wh) - r + (NA_WIN_H - 1)
        bias = rel_bias[:, dr_idx[:, None, None], dc_idx[None, :, :]].transpose(0, 2, 1, 3)
        s_loc = (jnp.einsum('bqhd,brqwhd->bhqrw', q_row, k_win).astype(jnp.float32) * scale
                 + bias.astype(jnp.float32))
        s_ctx = jnp.einsum('bqhd,bkhd->bhqk', q_row, kc).astype(jnp.float32) * scale
        s = jnp.concatenate([s_loc.reshape(b, NA_HEADS, GRID_W, n_loc), s_ctx], axis=-1)
        p = jax.nn.softmax(s, axis=-1).astype(v_win.dtype)
        p_loc = p[..., :n_loc].reshape(b, NA_HEADS, GRID_W, wh, NA_WIN_W)
        return (jnp.einsum('bhqrw,brqwhv->bqhv', p_loc, v_win)
                + jnp.einsum('bhqk,bkhv->bqhv', p[..., n_loc:], vc))

    o = lax.map(row_block, (jnp.arange(rows), jnp.moveaxis(grid(ql), 1, 0)))
    y_lat = jnp.moveaxis(o, 0, 1).reshape(b, n, NA_HEADS * NA_DH) @ w_out
    if not need_ctx:
        return None, y_lat
    y_ctx = softmax_attend(qc, kc, vc, scale).reshape(b, -1, NA_HEADS * NA_DH) @ w_out
    return y_ctx, y_lat

def split_qk_norm(t, g):
    return jnp.concatenate([rms_norm(t[..., :MLA_NOPE]), rms_norm(t[..., MLA_NOPE:])], axis=-1) * g.astype(t.dtype)

def rotate_rope_part(t):
    return jnp.concatenate([t[..., :MLA_NOPE], rope_2d(t[..., MLA_NOPE:])], axis=-1)

def mla_mixer(h_ctx, h_lat, w_down, q_norm_g, kv_norm_g, w_uq, w_ukv, qk_norm_q, qk_norm_k,
              w_out, need_ctx):
    def keys_values(z, rotate):
        b, n, _ = z.shape
        c_kv = z[..., MLA_Q_RANK:MLA_Q_RANK + MLA_KV_RANK]
        k_rope = z[..., MLA_Q_RANK + MLA_KV_RANK:]
        kv = (rms_norm_gain(c_kv, kv_norm_g) @ w_ukv).reshape(b, n, MLA_HEADS, MLA_NOPE + MLA_V)
        k_rope = jnp.broadcast_to(k_rope[:, :, None, :], (b, n, MLA_HEADS, MLA_ROPE))
        k = split_qk_norm(jnp.concatenate([kv[..., :MLA_NOPE], k_rope], axis=-1), qk_norm_k)
        return (rotate_rope_part(k) if rotate else k), kv[..., MLA_NOPE:]

    def queries(z, rotate):
        b, n, _ = z.shape
        q = (rms_norm_gain(z[..., :MLA_Q_RANK], q_norm_g) @ w_uq).reshape(b, n, MLA_HEADS, MLA_QK)
        q = split_qk_norm(q, qk_norm_q)
        return rotate_rope_part(q) if rotate else q

    scale = MLA_QK ** -0.5
    z_ctx = h_ctx @ w_down
    z_lat = h_lat @ w_down
    kc, vc = keys_values(z_ctx, False)
    kl, vl = keys_values(z_lat, True)
    ql = queries(z_lat, True)
    k_all = jnp.concatenate([kc, kl], axis=1)
    v_all = jnp.concatenate([vc, vl], axis=1)
    b, n = ql.shape[0], ql.shape[1]
    o = map_query_blocks(lambda qb: softmax_attend(qb, k_all, v_all, scale), ql)
    y_lat = o.reshape(b, n, MLA_HEADS * MLA_V) @ w_out
    if not need_ctx:
        return None, y_lat
    o_ctx = softmax_attend(queries(z_ctx, False), kc, vc, scale)
    return o_ctx.reshape(b, -1, MLA_HEADS * MLA_V) @ w_out, y_lat

def first_inputs(seed: int = 0) -> dict:
    key = jax.random.key(seed)
    keys = iter(jax.random.split(key, 40))
    f32 = jnp.float32

    def normal(shape, scale):
        return jax.random.normal(next(keys), shape, f32) * scale

    def gain(shape):
        return 1.0 + normal(shape, 0.02)

    d = D_MODEL
    n_ret, n_diff, n_na, n_mla = [len(range(m, DEPTH, N_MIXERS)) for m in range(N_MIXERS)]
    gam = 1.0 - 2.0 ** (-5.0 - np.arange(RET_HEADS, dtype=np.float32))
    decay_logit0 = jnp.asarray(np.log(gam / (1.0 - gam)), f32)
    ret_cols = 2 * RET_HEADS * RET_DK + 2 * RET_HEADS * RET_DV
    diff_cols = 2 * DIFF_HEADS * 2 * DIFF_DH + DIFF_HEADS * DIFF_DV
    mla_down_cols = MLA_Q_RANK + MLA_KV_RANK + MLA_ROPE
    return {
        'x': normal((BATCH, SEQ, d), 1.0),
        'c': normal((BATCH, d), 1.0),
        'ctx': normal((BATCH, CTX_LEN, d), 1.0),
        'c_ctx': normal((d,), 1.0),
        'ada_w': normal((DEPTH, d, ADA_CHUNKS * d), 0.5 * d ** -0.5),
        'ada_b': normal((DEPTH, ADA_CHUNKS * d), 0.02),
        'ret_w_in': normal((n_ret, d, ret_cols), d ** -0.5),
        'ret_decay_logit': decay_logit0 + normal((n_ret, 2, RET_HEADS), 0.1),
        'ret_norm_g': gain((n_ret, RET_HEADS * RET_DV)),
        'ret_w_out': normal((n_ret, RET_HEADS * RET_DV, d), (RET_HEADS * RET_DV) ** -0.5),
        'diff_w_in': normal((n_diff, d, diff_cols), d ** -0.5),
        'diff_q_norm_g': gain((n_diff, DIFF_DH)),
        'diff_k_norm_g': gain((n_diff, DIFF_DH)),
        'diff_lambda': normal((n_diff, 4, DIFF_DH), 0.1),
        'diff_subln_g': gain((n_diff, DIFF_DV)),
        'diff_w_out': normal((n_diff, DIFF_HEADS * DIFF_DV, d), (DIFF_HEADS * DIFF_DV) ** -0.5),
        'na_w_in': normal((n_na, d, 3 * NA_HEADS * NA_DH), d ** -0.5),
        'na_q_norm_g': gain((n_na, NA_DH)),
        'na_k_norm_g': gain((n_na, NA_DH)),
        'na_rel_bias': normal((n_na, NA_HEADS, 2 * NA_WIN_H - 1, 2 * NA_WIN_W - 1), 0.1),
        'na_w_out': normal((n_na, NA_HEADS * NA_DH, d), (NA_HEADS * NA_DH) ** -0.5),
        'mla_w_down': normal((n_mla, d, mla_down_cols), d ** -0.5),
        'mla_q_norm_g': gain((n_mla, MLA_Q_RANK)),
        'mla_kv_norm_g': gain((n_mla, MLA_KV_RANK)),
        'mla_w_uq': normal((n_mla, MLA_Q_RANK, MLA_HEADS * MLA_QK), MLA_Q_RANK ** -0.5),
        'mla_w_ukv': normal((n_mla, MLA_KV_RANK, MLA_HEADS * (MLA_NOPE + MLA_V)), MLA_KV_RANK ** -0.5),
        'mla_qk_norm_q': gain((n_mla, MLA_QK)),
        'mla_qk_norm_k': gain((n_mla, MLA_QK)),
        'mla_w_out': normal((n_mla, MLA_HEADS * MLA_V, d), (MLA_HEADS * MLA_V) ** -0.5),
        'ffn_w_in': normal((DEPTH, d, 2 * FFN_HIDDEN), d ** -0.5),
        'ffn_w_out': normal((DEPTH, FFN_HIDDEN, d), FFN_HIDDEN ** -0.5),
    }

def first_block(x, c, ctx, c_ctx, ada_w, ada_b,
              ret_w_in, ret_decay_logit, ret_norm_g, ret_w_out,
              diff_w_in, diff_q_norm_g, diff_k_norm_g, diff_lambda, diff_subln_g, diff_w_out,
              na_w_in, na_q_norm_g, na_k_norm_g, na_rel_bias, na_w_out,
              mla_w_down, mla_q_norm_g, mla_kv_norm_g, mla_w_uq, mla_w_ukv,
              mla_qk_norm_q, mla_qk_norm_k, mla_w_out,
              ffn_w_in, ffn_w_out):
    s_lat = jax.nn.silu(c)[:, None, :]
    s_ctx = jax.nn.silu(c_ctx)[None, None, :]
    x_lat, x_ctx = x, ctx
    for i in range(DEPTH):
        need_ctx = i < DEPTH - 1
        mod_l = jnp.split(s_lat @ ada_w[i] + ada_b[i], ADA_CHUNKS, axis=-1)
        mod_c = jnp.split(s_ctx @ ada_w[i] + ada_b[i], ADA_CHUNKS, axis=-1)
        h_lat = modulate(x_lat, mod_l[0], mod_l[1])
        h_ctx = modulate(x_ctx, mod_c[0], mod_c[1])
        kind, j = i % N_MIXERS, i // N_MIXERS
        if kind == 0:
            y_ctx, y_lat = retention_mixer(h_ctx, h_lat, ret_w_in[j], ret_decay_logit[j],
                                           ret_norm_g[j], ret_w_out[j], need_ctx)
        elif kind == 1:
            lambda_init = 0.8 - 0.6 * math.exp(-0.3 * i)
            y_ctx, y_lat = diff_attention_mixer(h_ctx, h_lat, diff_w_in[j], diff_q_norm_g[j],
                                                diff_k_norm_g[j], diff_lambda[j], diff_subln_g[j],
                                                diff_w_out[j], lambda_init, need_ctx)
        elif kind == 2:
            y_ctx, y_lat = neighborhood_mixer(h_ctx, h_lat, na_w_in[j], na_q_norm_g[j],
                                              na_k_norm_g[j], na_rel_bias[j], na_w_out[j], need_ctx)
        else:
            y_ctx, y_lat = mla_mixer(h_ctx, h_lat, mla_w_down[j], mla_q_norm_g[j], mla_kv_norm_g[j],
                                     mla_w_uq[j], mla_w_ukv[j], mla_qk_norm_q[j], mla_qk_norm_k[j],
                                     mla_w_out[j], need_ctx)
        x_lat = x_lat + mod_l[2] * y_lat
        x_lat = x_lat + mod_l[5] * swiglu(modulate(x_lat, mod_l[3], mod_l[4]), ffn_w_in[i], ffn_w_out[i])
        if need_ctx:
            x_ctx = x_ctx + mod_c[2] * y_ctx
            x_ctx = x_ctx + mod_c[5] * swiglu(modulate(x_ctx, mod_c[3], mod_c[4]), ffn_w_in[i], ffn_w_out[i])
    return x_lat


HEAD_DIM = 64
ROT_DIM = HEAD_DIM // 4
ROPE_THETA = 500000.0

A_Q_HEADS = 8
A_KV_HEADS = 2
A_WINDOW = 128

B_GROUPS = ((128, 1), (512, 4), (2048, 16))
N_B_GROUPS = 3
B_HEADS_PER_GROUP = 4

D_FF = 4 * D_MODEL
PLE_DIM = 256
N_BRANCHES = 2
LN_EPS = 1e-5
DEEPNORM_ALPHA = (2 * DEPTH) ** 0.25
DEEPNORM_BETA = (8 * DEPTH) ** -0.25

A_Q_W = A_Q_HEADS * HEAD_DIM
A_KV_W = A_KV_HEADS * HEAD_DIM
B_HEADS = N_B_GROUPS * B_HEADS_PER_GROUP
B_W = B_HEADS * HEAD_DIM
B_OUT_W = B_HEADS_PER_GROUP * HEAD_DIM
GATE_W = N_BRANCHES * D_MODEL
D_IN = A_Q_W + 2 * A_KV_W + 3 * B_W + GATE_W
IN_SPLITS = (A_Q_W, A_Q_W + A_KV_W, A_Q_W + 2 * A_KV_W,
             A_Q_W + 2 * A_KV_W + B_W, A_Q_W + 2 * A_KV_W + 2 * B_W,
             A_Q_W + 2 * A_KV_W + 3 * B_W)


def _layer_norm(x, g, b):
    xf = x.astype(jnp.float32)
    mu = jnp.mean(xf, axis=-1, keepdims=True)
    var = jnp.mean(jnp.square(xf - mu), axis=-1, keepdims=True)
    y = (xf - mu) * lax.rsqrt(var + LN_EPS) * g.astype(jnp.float32) + b.astype(jnp.float32)
    return y.astype(x.dtype)

def _rope_tables(seq):
    pos = jnp.arange(seq, dtype=jnp.float32)
    inv_freq = ROPE_THETA ** (-jnp.arange(0, ROT_DIM, 2, dtype=jnp.float32) / ROT_DIM)
    ang = pos[:, None] * inv_freq[None, :]
    return jnp.cos(ang), jnp.sin(ang)

def _rope(t, cos, sin):
    half = ROT_DIM // 2
    tf = t.astype(jnp.float32)
    t1, t2 = tf[..., :half], tf[..., half:ROT_DIM]
    c, s = cos[:, None, :], sin[:, None, :]
    out = jnp.concatenate([t1 * c - t2 * s, t2 * c + t1 * s, tf[..., ROT_DIM:]], axis=-1)
    return out.astype(t.dtype)

def _banded_attention(q, k, v, window, sink=None):
    n, seq, hq, dh = q.shape
    hkv = k.shape[2]
    grp = hq // hkv
    bs = window
    nblk = -(-seq // bs)
    lp = nblk * bs
    scale = 1.0 / math.sqrt(dh)
    qp = jnp.pad(q, ((0, 0), (0, lp - seq), (0, 0), (0, 0)))
    kp = jnp.pad(k, ((0, 0), (bs, lp - seq + bs), (0, 0), (0, 0))).astype(jnp.float32)
    vp = jnp.pad(v, ((0, 0), (bs, lp - seq + bs), (0, 0), (0, 0))).astype(jnp.float32)
    qb = qp.reshape(n, nblk, bs, hkv, grp, dh).transpose(1, 0, 2, 3, 4, 5)
    sink_b = None if sink is None else sink.astype(jnp.float32).reshape(1, hkv, grp, 1)

    def block(args):
        j, qj = args
        kj = lax.dynamic_slice_in_dim(kp, j * bs, 3 * bs, axis=1)
        vj = lax.dynamic_slice_in_dim(vp, j * bs, 3 * bs, axis=1)
        s = jnp.einsum('nqkgd,nskd->nkgqs', qj.astype(jnp.float32) * scale, kj)
        qpos = j * bs + jnp.arange(bs)
        kpos = j * bs - bs + jnp.arange(3 * bs)
        mask = (jnp.abs(qpos[:, None] - kpos[None, :]) <= window) & (kpos >= 0)[None, :] & (kpos < seq)[None, :]
        s = jnp.where(mask, s, -jnp.inf)
        m = jnp.max(s, axis=-1)
        if sink_b is not None:
            m = jnp.maximum(m, sink_b)
        e = jnp.exp(s - m[..., None])
        denom = jnp.sum(e, axis=-1)
        if sink_b is not None:
            denom = denom + jnp.exp(sink_b - m)
        o = jnp.einsum('nkgqs,nskd->nqkgd', e, vj) / denom.transpose(0, 3, 1, 2)[..., None]
        lse = (m + jnp.log(denom)).transpose(0, 3, 1, 2)
        return o, lse

    o, lse = lax.map(block, (jnp.arange(nblk), qb))
    o = o.transpose(1, 0, 2, 3, 4, 5).reshape(n, lp, hq, dh)[:, :seq].astype(q.dtype)
    lse = lse.transpose(1, 0, 2, 3, 4).reshape(n, lp, hq)[:, :seq]
    return o, lse

def _dilated_attention(q, k, v, window, dilation):
    n, seq, h, dh = q.shape
    r = dilation

    def sub(t):
        return t.reshape(n, seq // r, r, h, dh).transpose(0, 2, 1, 3, 4).reshape(n * r, seq // r, h, dh)

    o, lse = _banded_attention(sub(q), sub(k), sub(v), (window // 2) // r)
    o = o.reshape(n, r, seq // r, h, dh).transpose(0, 2, 1, 3, 4).reshape(n, seq, h, dh)
    lse = lse.reshape(n, r, seq // r, h).transpose(0, 2, 1, 3).reshape(n, seq, h)
    return o, lse

def _mixer_sublayer(x, cos, sin, w_in, b_gate, a_sink, w_branch_a, w_branch_b, w_out):
    bsz, seq, _ = x.shape
    proj = jnp.einsum('bsd,de->bse', x, w_in)
    qa, ka, va, qb, kb, vb, gl = jnp.split(proj, IN_SPLITS, axis=-1)

    qa = _rope(qa.reshape(bsz, seq, A_Q_HEADS, HEAD_DIM), cos, sin)
    ka = _rope(ka.reshape(bsz, seq, A_KV_HEADS, HEAD_DIM), cos, sin)
    va = va.reshape(bsz, seq, A_KV_HEADS, HEAD_DIM)
    oa, _ = _banded_attention(qa, ka, va, A_WINDOW, a_sink)
    ya = jnp.einsum('bse,ed->bsd', oa.reshape(bsz, seq, A_Q_W), w_branch_a)

    qb = _rope(qb.reshape(bsz, seq, B_HEADS, HEAD_DIM), cos, sin)
    kb = _rope(kb.reshape(bsz, seq, B_HEADS, HEAD_DIM), cos, sin)
    vb = vb.reshape(bsz, seq, B_HEADS, HEAD_DIM)
    outs, lses = [], []
    for g, (window, dil) in enumerate(B_GROUPS):
        hs = slice(g * B_HEADS_PER_GROUP, (g + 1) * B_HEADS_PER_GROUP)
        o, lse = _dilated_attention(qb[:, :, hs], kb[:, :, hs], vb[:, :, hs], window, dil)
        outs.append(o)
        lses.append(lse)
    wts = jax.nn.softmax(jnp.stack(lses), axis=0)
    ob = jnp.einsum('gbsh,gbshd->bshd', wts, jnp.stack(outs).astype(jnp.float32)).astype(x.dtype)
    yb = jnp.einsum('bse,ed->bsd', ob.reshape(bsz, seq, B_OUT_W), w_branch_b)

    gates = jax.nn.sigmoid((gl + b_gate).astype(jnp.float32)).astype(x.dtype)
    ga, gb = jnp.split(gates, N_BRANCHES, axis=-1)
    return jnp.einsum('bsd,de->bse', ga * ya + gb * yb, w_out)

def second_inputs(seed: int = 0) -> dict:
    key = jax.random.key(seed)
    ks = jax.random.split(key, 24)
    L, D = DEPTH, D_MODEL
    beta = DEEPNORM_BETA

    def dense(k, shape, fan_in, scale=1.0):
        return jax.random.normal(k, shape, jnp.float32) * (scale * fan_in ** -0.5)

    x = jax.random.normal(ks[0], (BATCH, SEQ, D), jnp.float32)
    p = jax.random.normal(ks[1], (DEPTH, BATCH, SEQ, PLE_DIM), jnp.float32)
    w_in = jnp.concatenate([
        dense(ks[2], (L, D, A_Q_W), D),
        dense(ks[3], (L, D, A_KV_W), D),
        dense(ks[4], (L, D, A_KV_W), D, beta),
        dense(ks[5], (L, D, B_W), D),
        dense(ks[6], (L, D, B_W), D),
        dense(ks[7], (L, D, B_W), D, beta),
        dense(ks[8], (L, D, GATE_W), D),
    ], axis=-1)
    b_gate = 0.1 * jax.random.normal(ks[9], (L, GATE_W), jnp.float32)
    a_sink = 0.5 * jax.random.normal(ks[10], (L, A_Q_HEADS), jnp.float32)
    w_branch_a = dense(ks[11], (L, A_Q_W, D), A_Q_W, beta)
    w_branch_b = dense(ks[12], (L, B_OUT_W, D), B_OUT_W, beta)
    w_out = dense(ks[13], (L, D, D), D, beta)
    ln1_g = 1.0 + 0.02 * jax.random.normal(ks[14], (L, D), jnp.float32)
    ln1_b = 0.02 * jax.random.normal(ks[15], (L, D), jnp.float32)
    w_up = dense(ks[16], (L, D, D_FF), D)
    w_down = dense(ks[17], (L, D_FF, D), D_FF, beta)
    w_ple_gate = dense(ks[18], (L, D, D), D)
    b_ple_gate = 0.1 * jax.random.normal(ks[19], (L, D), jnp.float32)
    w_ple = dense(ks[20], (L, PLE_DIM, D), PLE_DIM, beta)
    ln2_g = 1.0 + 0.02 * jax.random.normal(ks[21], (L, D), jnp.float32)
    ln2_b = 0.02 * jax.random.normal(ks[22], (L, D), jnp.float32)
    return {"x": x, "p": p, "w_in": w_in, "b_gate": b_gate, "a_sink": a_sink,
            "w_branch_a": w_branch_a, "w_branch_b": w_branch_b, "w_out": w_out,
            "ln1_g": ln1_g, "ln1_b": ln1_b, "w_up": w_up, "w_down": w_down,
            "w_ple_gate": w_ple_gate, "b_ple_gate": b_ple_gate, "w_ple": w_ple,
            "ln2_g": ln2_g, "ln2_b": ln2_b}

def second_block(x, p, w_in, b_gate, a_sink, w_branch_a, w_branch_b, w_out,
              ln1_g, ln1_b, w_up, w_down, w_ple_gate, b_ple_gate, w_ple,
              ln2_g, ln2_b):
    cos, sin = _rope_tables(x.shape[1])
    for i in range(DEPTH):
        h = _mixer_sublayer(x, cos, sin, w_in[i], b_gate[i], a_sink[i],
                            w_branch_a[i], w_branch_b[i], w_out[i])
        x = _layer_norm(DEEPNORM_ALPHA * x + h, ln1_g[i], ln1_b[i])
        mlp = jnp.einsum('bsf,fd->bsd', jnp.square(jax.nn.relu(jnp.einsum('bsd,df->bsf', x, w_up[i]))), w_down[i])
        gate = jax.nn.sigmoid((jnp.einsum('bsd,de->bse', x, w_ple_gate[i]) + b_ple_gate[i]).astype(jnp.float32)).astype(x.dtype)
        ple = gate * jnp.einsum('bsr,rd->bsd', p[i], w_ple[i])
        x = _layer_norm(DEEPNORM_ALPHA * x + mlp + ple, ln2_g[i], ln2_b[i])
    return x


def setup_inputs(seed=0):
    out = dict(first_inputs(seed))
    for name, value in second_inputs(seed + 1).items():
        if name != "x":
            out[name + "_2"] = value
    return out


def reference(
    x, c, ctx, c_ctx, ada_w, ada_b, ret_w_in, ret_decay_logit, ret_norm_g, ret_w_out, diff_w_in,
    diff_q_norm_g, diff_k_norm_g, diff_lambda, diff_subln_g, diff_w_out, na_w_in, na_q_norm_g,
    na_k_norm_g, na_rel_bias, na_w_out, mla_w_down, mla_q_norm_g, mla_kv_norm_g, mla_w_uq,
    mla_w_ukv, mla_qk_norm_q, mla_qk_norm_k, mla_w_out, ffn_w_in, ffn_w_out, p_2, w_in_2,
    b_gate_2, a_sink_2, w_branch_a_2, w_branch_b_2, w_out_2, ln1_g_2, ln1_b_2, w_up_2, w_down_2,
    w_ple_gate_2, b_ple_gate_2, w_ple_2, ln2_g_2, ln2_b_2,
):
    x = first_block(
        x, c, ctx, c_ctx, ada_w, ada_b, ret_w_in, ret_decay_logit, ret_norm_g, ret_w_out,
        diff_w_in, diff_q_norm_g, diff_k_norm_g, diff_lambda, diff_subln_g, diff_w_out, na_w_in,
        na_q_norm_g, na_k_norm_g, na_rel_bias, na_w_out, mla_w_down, mla_q_norm_g,
        mla_kv_norm_g, mla_w_uq, mla_w_ukv, mla_qk_norm_q, mla_qk_norm_k, mla_w_out, ffn_w_in,
        ffn_w_out,
    )
    return second_block(
        x, p_2, w_in_2, b_gate_2, a_sink_2, w_branch_a_2, w_branch_b_2, w_out_2, ln1_g_2,
        ln1_b_2, w_up_2, w_down_2, w_ple_gate_2, b_ple_gate_2, w_ple_2, ln2_g_2, ln2_b_2,
    )


_drawn_inputs = setup_inputs


def setup_inputs(seed=0):
    import zlib

    import numpy as np

    out = dict(_drawn_inputs(seed))
    spreads = {}
    factors = {'ret_norm_g': 8.0,
     'diff_q_norm_g': 8.0,
     'diff_k_norm_g': 8.0,
     'diff_lambda': 8.0,
     'diff_subln_g': 28.014,
     'b_gate_2': 8.0,
     'a_sink_2': 59.026,
     'w_branch_a_2': 3.319,
     'w_branch_b_2': 4.367,
     'b_ple_gate_2': 5.841}
    for name, (base, spread) in spreads.items():
        noise = np.random.default_rng([zlib.crc32(name.encode()), seed]).standard_normal(out[name].shape)
        drawn = base * np.exp(spread * noise) if base else spread * noise
        out[name] = __import__('jax').numpy.asarray(drawn.astype(out[name].dtype))
    for name, factor in factors.items():
        out[name] = (out[name] * factor).astype(out[name].dtype)
    return out
```

```python
import math
from contextlib import ExitStack

import concourse.bass as bass
from concourse import mybir

F32 = mybir.dt.float32
F32R = mybir.dt.float32r
ALU = mybir.AluOpType
ACT = mybir.ActivationFunctionType
AX = mybir.AxisListType

P = 128
D = 1024
KD = D // P
SEQ = 256
EPS = 1e-6
LN_EPS = 1e-5
RH, RDK, RDV = 4, 256, 512
DH, DDH = 8, 64
LAMBDA_INIT = 0.8 - 0.6 * math.exp(-0.3 * 1)
FFN = 2816
ALPHA = 4 ** 0.25
MASKED = -1e30

RAW_SLOTS = 4
SPLIT_SLOTS = 2
MOD_UNITS = 48
UNIT = 2048

C_IDENT = 0
C_DIST = C_IDENT + P
C_RC = C_DIST + 384
C_RS = C_RC + 512
C_SEL = C_RS + 512
C_DC = C_SEL + 2
C_DS = C_DC + 128
C_BC = C_DS + 128
C_BS = C_BC + 32
C_MA = C_BS + 32
C_MB = C_MA + 512
C_ALL = C_MB + 1024
C_HELD = C_DC
C2_D = C_RC
C2_GAIN = C2_D + (C_MA - C_DC)

V_ADA, V_C, V_CC, V_NG, V_BG, V_SUB = 0, 96, 104, 112, 128, 160


def plan():
    head = [("qk", 2), ("oT", 0), ("v", 2), ("qkT", 0), ("scores", 0), ("gate", 2), ("pv", 0)]
    cells = [("s", 0), ("s", 0), ("pT", 0), ("pv", 0)] + [("s", 0), ("pT", 0), ("pv", 0)] * 2 + [("pT", 0), ("pv", 0)]
    half = [("q", 2), ("k", 2), ("v", 2), ("qT", 0), ("kT", 0)] + cells + [("oT", 0)]
    first = [("cols", 0)] + [("mod rows", 8), ("mod cols", 0)] * 6 + [("xT", 0)] * 2 + head[:1] + head[2:] + head * (RH - 1) + [("oT", 0)]
    first += [("row gates", 0)] + [("out", 2)] * 4
    first += [("xT", 0)] * 2 + [("ffn", 2)] * 5 + [("ffn", 1)] + [("row gates", 0)] + [("out", 3)] * 2
    first += [("ffn", 2)] * 5 + [("ffn", 1)] + [("out", 3)] * 2
    first += [("xT", 0)] * 2 + half * 2 + [("row gates", 0)] + [("out", 2)] * 2
    first += [("xT", 0)] + [("ffn", 4)] * 5 + [("ffn", 2)] + [("row gates", 0)] + [("out", 6)] * 2
    layer = [("xT", 0)] + [("in", 2), ("inT", 0)] * 2 + [("s", 0), ("in", 2), ("pT", 0), ("pv", 0)] * 2
    layer += [("inT", 0)] + [("in", 2), ("inT", 0)] * 2
    layer += cells + [("gates", 4)] * 2 + [("branch a", 2), ("branch b", 1)]
    layer += [("out", 2)] * 2 + [("xT", 0)] + [("ple gate", 2)] * 2 + [("ple", 1)] + [("up", 4)] * 4 + [("down", 8)] * 2
    return first, layer


IN_ORDER = (0, 1, 5, 2, 3, 4)
FIRST, LAYER = plan()
PLAN = FIRST + LAYER * 2
UNITS_BEFORE = [sum(n for _, n in PLAN[:i]) for i in range(len(PLAN) + 1)]
STAGES_BEFORE = [sum(n == 0 for _, n in PLAN[:i]) for i in range(len(PLAN) + 1)]
TOTAL_UNITS = UNITS_BEFORE[-1]
LAYER_UNITS = sum(n for _, n in LAYER)


class Side:

    def __init__(self):
        self.unit = self.step = self.now = 0
        self.split = MOD_UNITS
        self.seen = {}

    def count(self, name):
        return self.seen.get(name, 0)

    def next(self, name, n=1):
        self.seen[name] = self.count(name) + n
        return self.seen[name]

    def begin(self, name):
        assert PLAN[self.step][0] == name, (self.step, PLAN[self.step], name)
        self.now = self.step
        self.step += 1

    def units(self):
        assert PLAN[self.now][1]
        return UNITS_BEFORE[self.now + 1]

    def stages(self, step=None):
        step = self.now if step is None else step
        assert not PLAN[step][1]
        return STAGES_BEFORE[step + 1]

    def reads(self, step=None):
        return (self.now if step is None else step) // 2 + 1


def sizes():
    out = [UNIT] * TOTAL_UNITS
    u = UNITS_BEFORE[0]
    i = 0
    for s, (name, n) in enumerate(PLAN):
        if name == "out" and n == 3:
            out[UNITS_BEFORE[s + 1] - 1] = 3 * 512
        if name == "out" and n == 6:
            out[UNITS_BEFORE[s + 1] - 1] = 2 * 512
    return out


SIZES = sizes()



def build(nc, A, out):
    ctx = ExitStack()
    with ctx:
        def sb(name, shape, dt=F32):
            return ctx.enter_context(nc.sbuf_tensor(name, shape, dt))

        raw = sb("raw", [P, RAW_SLOTS, UNIT])
        w_hi = sb("w_hi", [P, SPLIT_SLOTS, UNIT], F32R)
        w_lo = sb("w_lo", [P, SPLIT_SLOTS, UNIT], F32R)
        hT_hi = sb("hT_hi", [P, KD, 512], F32R)
        hT_lo = sb("hT_lo", [P, KD, 512], F32R)
        big_hi = sb("big_hi", [P, 8192], F32R)
        big_lo = sb("big_lo", [P, 8192], F32R)
        const = sb("const", [P, C_HELD])
        cols = sb("cols", [P, 161])
        mod = sb("mod", [P, 2, 48, 2])
        ones = sb("ones", [P, P])
        dec = sb("dec", [P, 5, 8])
        lam = sb("lam", [P, 4])
        st = sb("st", [P, 176])
        ARENA = 9984
        arena = sb("arena", [P, ARENA])
        ps = ctx.enter_context(nc.psum_tensor("ps", [P, 8, 512], F32))

        names = ["unit_used", "pe_stage", "psum_free0", "psum_free1", "hi_ready", "lo_ready", "out_stored"]
        names += ["const_in", "vec_in", "x_in", "dec_in", "lam_in", "bias_in", "const2_in", "mask_in", "sink_in",
                  "p_in", "ln1_in", "ln2_in", "bple_in"]
        names += ["ones_set", "silu_c", "dec_abs", "dec_exp", "dec_ready", "lam_arg", "lam_exp",
                  "x_ready", "sq_ready", "rv_ready", "rs_ready", "xn_ready", "hT_ready",
                  "roped", "in_ready", "mask_arg", "mask_exp", "var_ready", "rstd_ready", "on_hi", "on_lo",
                  "diag_ready", "silu_ready", "hid_hi", "hid_lo", "qk_sq", "qk_rt", "qk_ready", "v_hi",
                  "max_ready", "p_exp", "p_ready", "pT_hi", "o_sq", "o_rt", "o_ready", "oT_hi", "oT_lo",
                  "mix_ready", "mix_hi", "mix_lo", "relu_ready", "sqr_ready", "gl_ready", "gs_ready",
                  "ple_hi", "xT_hi", "ln_var", "ln_rstd", "x_next"]
        sem = {n: ctx.enter_context(nc.semaphore(n)) for n in names}
        psum_free = [sem["psum_free0"], sem["psum_free1"]]
        unit_in = [ctx.enter_context(nc.semaphore(f"unit_in{r}")) for r in range(RAW_SLOTS)]
        ident = const[:, C_IDENT:C_IDENT + P]
        dist = const[:, C_DIST:C_DIST + 384]
        select = const[:, C_SEL:C_SEL + 2]

        def half(step):
            return ps[:, 4 * (step % 2):4 * (step % 2) + 4, :]

        def at(a, *dims):
            n = math.prod(dims)
            assert a + n <= ARENA
            v = arena[:, a:a + n]
            if len(dims) == 2:
                v = v.rearrange("p (a b) -> p a b", a=dims[0])
            if len(dims) == 3:
                v = v.rearrange("p (a b c) -> p a b c", a=dims[0], b=dims[1])
            return v

        def big(t, a, *dims):
            n = math.prod(dims)
            v = t[:, a:a + n]
            if len(dims) == 2:
                v = v.rearrange("p (a b) -> p a b", a=dims[0])
            if len(dims) == 3:
                v = v.rearrange("p (a b c) -> p a b c", a=dims[0], b=dims[1])
            return v

        X4, XN4 = at(0, 4, 1024), at(4096, 4, 1024)
        MROW, vec, vec2, lvec = at(6144, 2048), at(8192, 128), at(8320, 128), at(8448, 256)
        lprod = at(8704, 2, 64)
        GATE, DIAG, TMP = at(4096, 2, 1024), at(6144, 2048), at(6144, 4, 512)
        SILU = at(8192, 1024)
        QK, PT, QKT, ON = at(0, 4, 512), at(0, 6, 256), at(2048, 4, 512), at(2048, 4, 512)
        VN, GT, ROPE = at(4096, 4, 512), at(6144, 4, 512), at(9728, 256)
        G1, G2, T1, T2 = (at(8192 + 384 * n, 384) for n in range(4))
        KN, QN, SQ, DQT, DKT = at(2048, 4, 512), at(5120, 2, 512), at(4096, 1024), at(6144, 4, 256), at(7168, 4, 512)
        DP, DO = at(2048, 4, 512), at(4096, 2, 512)
        X2, NAT, KDUP = at(0, 2, 1024), at(2048, 2, 512), at(3072, 2, 256)
        QAT, KAT, QBT, KBT = at(3584, 4, 256), at(4608, 2, 256), at(5120, 6, 256), at(6656, 6, 256)
        MB, SINK, PA = at(8704, 1024), at(9728, 8), at(6656, 4, 512)
        MA = const[:, C2_GAIN + 128:C2_GAIN + 640]
        PIN = MA.rearrange("p (t n) -> p t n", t=2)
        PB = [at(2048, 3, 512), at(3584, 3, 512)]
        GS, MIX = at(2048, 16, 256), at(6144, 8, 256)
        LN1G, LN1B = at(2048, 1024), at(3072, 1024)
        PLE, BPLE, HID = at(4096, 2, 1024), at(6144, 1024), at(7168, 2048)

        V0, PT0, OT0, PIN0 = 0, 4096, 6144, 7680

        block = ctx.enter_context(nc.Block())

        def kpn(w):
            return w.rearrange("(k p) n -> p k n", p=P)

        def bcast(row, n):
            return row.to_broadcast([P, n])

        @block.sync
        def _(sp):
            s = Side()

            def load(view, n, part):
                u = s.unit
                assert n == SIZES[u], (u, n, SIZES[u])
                if u >= MOD_UNITS + RAW_SLOTS:
                    sp.wait_ge(sem["lo_ready"], u - RAW_SLOTS + 1 - MOD_UNITS)
                elif u >= RAW_SLOTS:
                    sp.wait_ge(sem["unit_used"], u - RAW_SLOTS + 1)
                for j in range(2):
                    sp.dma_start(view(raw[:, u % RAW_SLOTS, 0:n], j), part(j)).then_inc(unit_in[u % RAW_SLOTS], 16)
                s.unit += 1

            def by_k(w, k0, nk, c0, n):
                b = [0, nk // 2, nk]
                load(lambda d, j: d.rearrange("p (k n) -> p k n", k=nk)[:, b[j]:b[j + 1], :], nk * n,
                     lambda j: kpn(w)[:, k0 + b[j]:k0 + b[j + 1], c0:c0 + n])

            def pair(w, c0, gap):
                load(lambda d, j: d.rearrange("p (k g n) -> p k g n", k=KD, g=2)[:, :, j, :], UNIT,
                     lambda j: kpn(w)[:, :, c0 + j * gap:c0 + j * gap + P])

            for d in range(2):
                for g in range(12):
                    by_k(A["ada_w"][d], 0, 4, g * 512, 512)
                    by_k(A["ada_w"][d], 4, 4, g * 512, 512)
            w = A["ret_w_in"][0]
            for h in range(RH):
                by_k(w, 0, KD, h * RDK, 256)
                by_k(w, 0, KD, RH * RDK + h * RDK, 256)
                for k0 in (0, 4):
                    by_k(w, k0, 4, 2 * RH * RDK + h * RDV, 512)
                for c in (0, 256):
                    by_k(w, 0, KD, 2 * RH * RDK + RH * RDV + h * RDV + c, 256)
            for kh in (0, 8):
                for c0 in (0, 512):
                    for k0 in (0, 4):
                        by_k(A["ret_w_out"][0], kh + k0, 4, c0, 512)
            for hf in range(2):
                for c in range(11):
                    pair(A["ffn_w_in"][0], (hf * 11 + c) * P, FFN)
                for c0 in (0, 512):
                    for k0, nk in ((0, 4), (4, 4), (8, 3)):
                        by_k(A["ffn_w_out"][0], hf * 11 + k0, nk, c0, 512)
            for hf in range(2):
                for part in range(3):
                    for k0 in (0, 4):
                        by_k(A["diff_w_in"][0], k0, 4, part * D + hf * 512, 512)
            for c0 in (0, 512):
                for k0 in (0, 4):
                    by_k(A["diff_w_out"][0], k0, 4, c0, 512)
            for c in range(22):
                pair(A["ffn_w_in"][1], c * P, FFN)
            for c0 in (0, 512):
                for k0 in range(0, 22, 4):
                    by_k(A["ffn_w_out"][1], k0, min(4, 22 - k0), c0, 512)

            def layer(i):
                wi = A["w_in_2"][i]
                for c in IN_ORDER:
                    for k0 in (0, 4):
                        by_k(wi, k0, 4, c * 512, 512)
                for c0 in range(3072, 5120, 256):
                    by_k(wi, 0, KD, c0, 256)
                for c0 in (0, 512):
                    by_k(A["w_branch_a_2"][i], 0, 4, c0, 512)
                by_k(A["w_branch_b_2"][i], 0, 2, 0, 1024)
                for name in ("w_out_2", "w_ple_gate_2"):
                    for c0 in (0, 512):
                        for k0 in (0, 4):
                            by_k(A[name][i], k0, 4, c0, 512)
                by_k(A["w_ple_2"][i], 0, 2, 0, 1024)
                for c0 in range(0, 4096, 256):
                    by_k(A["w_up_2"][i], 0, KD, c0, 256)
                for c0 in (0, 512):
                    for k0 in range(0, 32, 4):
                        by_k(A["w_down_2"][i], k0, 4, c0, 512)

            for i in range(2):
                layer(i)
            assert s.unit == TOTAL_UNITS
            sp.wait_ge(sem["x_next"], s.next("x_next", 1 + 2 * 2))
            sp.dma_start(out[0].rearrange("(t p) n -> p t n", p=P), X2).then_inc(sem["out_stored"], 16)
            sp.wait_ge(sem["out_stored"], 16)

        @block.gpsimd
        def _(pool):
            s = Side()

            def fetch(dst, src, name):
                pool.dma_start(dst, src).then_inc(name, 16)

            pool.memset(ones[:], 1.0).then_inc(sem["ones_set"], 1)
            fetch(const[:], A["table"][:, 0:C_HELD], sem["const_in"])
            fetch(vec[0:96], A["ada_b"].rearrange("a (j n) -> (a j) n", n=P), sem["vec_in"])
            fetch(vec[96:104], A["c"][0].rearrange("(j n) -> j n", n=P), sem["vec_in"])
            fetch(vec[104:112], A["c_ctx"].rearrange("(j n) -> j n", n=P), sem["vec_in"])
            fetch(vec[112:128], A["ret_norm_g"][0].rearrange("(j n) -> j n", n=P), sem["vec_in"])
            fetch(vec2[0:32], A["b_gate_2"].rearrange("a (j n) -> (a j) n", n=P), sem["vec_in"])
            fetch(vec2[32:33], A["diff_subln_g"], sem["vec_in"])
            fetch(dec[:, 0, :], bcast(A["ret_decay_logit"].rearrange("a b c -> a (b c)"), 8), sem["dec_in"])
            fetch(lvec[:, :], bcast(A["diff_lambda"].rearrange("a b c -> a (b c)"), 256), sem["lam_in"])

            def load_x():
                fetch(X4[:, 0:2, :], A["x"][0].rearrange("(t p) n -> p t n", p=P), sem["x_in"])
                fetch(X4[:, 2:4, :], A["ctx"][0].rearrange("(t p) n -> p t n", p=P), sem["x_in"])

            load_x()
            for g in range(6):
                if g:
                    pool.wait_ge(sem["pe_stage"], s.stages(2 * g))
                d, c = divmod(g, 3)
                fetch(MROW[2:3, :], A["ada_b"][d:d + 1, c * 2048:(c + 1) * 2048], sem["bias_in"])
            pool.wait_ge(sem["pe_stage"], s.stages(14 + 7 * RH))
            load_x()
            fetch(const[:, C2_D:C2_D + C_MA - C_DC], A["table"][:, C_DC:C_MA], sem["const2_in"])
            fetch(const[:, C2_GAIN:C2_GAIN + 64], bcast(A["diff_q_norm_g"], 64), sem["const2_in"])
            fetch(const[:, C2_GAIN + 64:C2_GAIN + 128], bcast(A["diff_k_norm_g"], 64), sem["const2_in"])
            base = len(FIRST)
            for i in range(2):
                pool.wait_ge(sem["x_next"], s.next("x_next"))
                fetch(MB[:, :], A["table"][:, C_MB:C_MB + 1024], sem["mask_in"])
                fetch(MA[:, :], A["table"][:, C_MA:C_MA + 512], sem["mask_in"])
                fetch(SINK[:, :], bcast(A["a_sink_2"][i:i + 1, :], 8), sem["sink_in"])
                pool.wait_ge(psum_free[(base + LAYER.index(("s", 0)) + 4) % 2], s.reads(base + LAYER.index(("s", 0)) + 4))
                fetch(PIN, A["p_2"][i, 0].rearrange("(t p) n -> p t n", p=P), sem["p_in"])
                pool.wait_ge(sem["mix_ready"], s.next("mix_ready"))
                fetch(LN1G[:, :], bcast(A["ln1_g_2"][i:i + 1, :], 1024), sem["ln1_in"])
                fetch(LN1B[:, :], bcast(A["ln1_b_2"][i:i + 1, :], 1024), sem["ln1_in"])
                pool.wait_ge(sem["mix_lo"], s.next("mix_lo"))
                fetch(BPLE[:, :], bcast(A["b_ple_gate_2"][i:i + 1, :], 1024), sem["bple_in"])
                pool.wait_ge(sem["x_next"], s.next("x_next"))
                fetch(LN1G[:, :], bcast(A["ln2_g_2"][i:i + 1, :], 1024), sem["ln2_in"])
                fetch(LN1B[:, :], bcast(A["ln2_b_2"][i:i + 1, :], 1024), sem["ln2_in"])
                base += len(LAYER)

        @block.scalar
        def _(act):
            s = Side()

            def split(n):
                while s.split < min(n, TOTAL_UNITS):
                    u = s.split
                    m = SIZES[u]
                    act.wait_ge(unit_in[u % RAW_SLOTS], 32 * (u // RAW_SLOTS + 1))
                    if u >= SPLIT_SLOTS:
                        act.wait_ge(sem["unit_used"], u - SPLIT_SLOTS + 1)
                    act.activation(w_hi[:, u % SPLIT_SLOTS, 0:m], raw[:, u % RAW_SLOTS, 0:m], ACT.Copy).then_inc(sem["hi_ready"], 1)
                    s.split += 1

            def begin(name):
                s.begin(name)
                split(UNITS_BEFORE[s.now + 1] + SPLIT_SLOTS)
                act.drain()
                return half(s.now)

            def modulated(d, shift, scale, tb, loaded=False):
                X, XN = (X4, XN4)
                if loaded:
                    act.wait_ge(sem["x_in"], s.next("x_in", 32))
                else:
                    act.wait_ge(sem["x_ready"], s.next("x_ready"))
                for t in range(tb):
                    i = act.activation(XN[:, t, :], X[:, t, :], ACT.Square, accum_out=st[:, t:t + 1])
                i.then_inc(sem["sq_ready"], 1)
                act.wait_ge(sem["rv_ready"], s.next("rv_ready"))
                act.activation(st[:, 8:8 + tb], st[:, 4:4 + tb], ACT.Sqrt).then_inc(sem["rs_ready"], 1)
                per = 16 // tb
                for c0 in range(0, KD, per):
                    b = begin("xT").rearrange("p b n -> p (b n)").rearrange("p (c t n) -> p c t n", c=per, t=tb)
                    act.wait_ge(sem["pe_stage"], s.stages())
                    for c in range(per):
                        for m in range(tb // 2):
                            f = c0 + c
                            i = act.activation(XN[:, 2 * m:2 * m + 2, f * P:(f + 1) * P], b[:, c, 2 * m:2 * m + 2, :], ACT.Identity,
                                               bias=mod[:, d, shift * 8 + f, m:m + 1], scale=mod[:, d, scale * 8 + f, m:m + 1])
                    i.then_inc(psum_free[s.now % 2], 1)

            def gates():
                b = begin("row gates")
                act.wait_ge(sem["pe_stage"], s.stages())
                act.activation(GATE.rearrange("p a b -> p (a b)"), b.rearrange("p b n -> p (b n)"), ACT.Copy).then_inc(psum_free[s.now % 2], 1)

            def gates1():
                b = begin("row gates")
                act.wait_ge(sem["pe_stage"], s.stages())
                act.activation(GATE[:, 0, :], b[:, 0:2, :].rearrange("p b n -> p (b n)"), ACT.Copy).then_inc(psum_free[s.now % 2], 1)

            def ffn(chunks, per, T, first=True):
                c0 = 0
                while c0 < chunks:
                    n = min(per, chunks - c0)
                    b = begin("ffn")
                    act.wait_ge(sem["unit_used"], s.units())
                    if T == 512:
                        a = b.rearrange("p (c g) n -> p c g n", g=2)[:, 0:n, 0, :]
                    else:
                        a = b.rearrange("p c (g n) -> p c g n", g=2)[:, 0:n, 0, :]
                    if s.count("hid_lo"):
                        act.wait_ge(sem["hid_lo"], s.count("hid_lo"))
                    s.next("hid_lo")
                    act.activation(SILU[:, 0:n * T].rearrange("p (c n) -> p c n", c=n), a, ACT.Silu).then_inc(sem["silu_ready"], 1)
                    act.wait_ge(psum_free[s.now % 2], s.reads())
                    act.activation(big_hi[:, c0 * T:(c0 + n) * T], SILU[:, 0:n * T], ACT.Copy).then_inc(sem["hid_hi"], 1)
                    c0 += n

            act.wait_ge(sem["dec_abs"], s.next("dec_abs"))
            act.activation(dec[:, 2, :], dec[:, 1, :], ACT.Exp, scale=-1.0).then_inc(sem["dec_exp"], 1)
            act.wait_ge(sem["lam_arg"], s.next("lam_arg"))
            act.activation(lam[:, 2:4], lam[:, 0:2], ACT.Exp).then_inc(sem["lam_exp"], 1)
            begin("cols")
            act.wait_ge(psum_free[s.now % 2], s.reads())
            act.activation(st[:, 16:32], cols[:, V_C:V_C + 16], ACT.Silu).then_inc(sem["silu_c"], 1)
            for g in range(6):
                b = begin("mod rows")
                act.wait_ge(sem["unit_used"], s.units())
                act.activation(MROW[0:2, :], b[0:2].rearrange("p b n -> p (b n)"), ACT.Copy).then_inc(psum_free[s.now % 2], 1)
                begin("mod cols")
            act.wait_ge(psum_free[s.now % 2], s.reads())
            modulated(0, 0, 1, 4, loaded=True)

            def out_hi(h):
                begin("oT")
                act.wait_ge(psum_free[s.now % 2], s.reads())
                act.activation(big_hi[:, h * 2048:(h + 1) * 2048], GT.rearrange("p a b -> p (a b)"), ACT.Copy).then_inc(sem["on_hi"], 1)

            for h in range(RH):
                b = begin("qk")
                act.wait_ge(sem["unit_used"], s.units())
                act.activation(QK[:, :, 0:256], b[:, :, 0:256], ACT.Copy)
                act.activation(QK[:, :, 256:512], b[:, :, 256:512], ACT.Copy, scale=RDK ** -0.5).then_inc(psum_free[s.now % 2], 1)
                act.wait_ge(sem["mask_arg"], s.next("mask_arg"))
                if h == 0:
                    act.wait_ge(sem["dec_ready"], s.next("dec_ready"))
                f, bw = dec[:, 0, h:h + 1], dec[:, 0, 4 + h:5 + h]
                act.activation(G2, dist, ACT.Exp, scale=f, bias=dec[:, 2, h:h + 1])
                act.activation(G1, dist, ACT.Exp, scale=dec[:, 1, 4 + h:5 + h], bias=dec[:, 2, 4 + h:5 + h])
                act.activation(T1, T1, ACT.Exp, scale=f)
                act.activation(T2, T2, ACT.Exp, scale=bw).then_inc(sem["mask_exp"], 1)
                if h:
                    out_hi(h - 1)
                b = begin("v")
                act.wait_ge(sem["unit_used"], s.units())
                act.activation(VN[:, :, :], b, ACT.Copy).then_inc(psum_free[s.now % 2], 1)
                b = begin("qkT")
                act.wait_ge(sem["pe_stage"], s.stages())
                act.activation(QKT[:, :, :], b, ACT.Copy).then_inc(psum_free[s.now % 2], 1)
                begin("scores")
                b = begin("gate")
                act.wait_ge(sem["unit_used"], s.units())
                if s.count("on_lo"):
                    act.wait_ge(sem["on_lo"], s.count("on_lo"))
                s.next("on_lo")
                act.activation(GT[:, :, :], b, ACT.Silu).then_inc(psum_free[s.now % 2], 1)
                begin("pv")
                act.wait_ge(sem["var_ready"], s.next("var_ready"))
                act.activation(st[:, 8:12], st[:, 4:8], ACT.Sqrt).then_inc(sem["rstd_ready"], 1)
            out_hi(RH - 1)

            def out_strips(n):
                for _ in range(n):
                    begin("out")

            gates()
            out_strips(4)
            modulated(0, 3, 4, 4)
            ffn(11, 2, 512)
            gates()
            out_strips(2)
            ffn(11, 2, 512)
            out_strips(2)
            modulated(1, 0, 1, 4)

            for hf in range(2):
                b = begin("q")
                act.wait_ge(sem["unit_used"], s.units())
                act.activation(QN, b[:, 0:2, :], ACT.Copy).then_inc(psum_free[s.now % 2], 1)
                act.wait_ge(sem["qk_sq"], s.next("qk_sq"))
                act.activation(st[:, 64:80], st[:, 32:48], ACT.Sqrt).then_inc(sem["qk_rt"], 1)
                b = begin("k")
                act.wait_ge(sem["unit_used"], s.units())
                act.activation(KN, b, ACT.Copy).then_inc(psum_free[s.now % 2], 1)
                act.wait_ge(sem["qk_sq"], s.next("qk_sq"))
                act.activation(st[:, 64:96], st[:, 32:64], ACT.Sqrt).then_inc(sem["qk_rt"], 1)
                b = begin("v")
                act.wait_ge(sem["unit_used"], s.units())
                act.activation(big(big_hi, 2048, 4, 512), b, ACT.Copy).then_inc(sem["v_hi"], 1)
                b = begin("qT")
                act.wait_ge(sem["pe_stage"], s.stages())
                act.activation(DQT.rearrange("p a b -> p (a b)"), b[:, 0:2, :].rearrange("p a b -> p (a b)"), ACT.Copy).then_inc(psum_free[s.now % 2], 1)
                b = begin("kT")
                act.wait_ge(sem["pe_stage"], s.stages())
                act.activation(DKT[:, :, :], b, ACT.Copy).then_inc(psum_free[s.now % 2], 1)
                first_s = s.step

                def exponentials(b, step):
                    act.wait_ge(sem["max_ready"], s.next("max_ready"))
                    for m in range(4):
                        i = act.activation(DP[:, m, :], b[:, m, :], ACT.Exp, scale=DDH ** -0.5,
                                           bias=st[:, 100 + m:101 + m], accum_out=st[:, 104 + m:105 + m])
                    i.then_inc(psum_free[step % 2], 1)

                b = begin("s")
                act.wait_ge(sem["pe_stage"], s.stages())
                exponentials(b, s.now)
                for h in range(4):
                    if h < 3:
                        scores, scores_step = begin("s"), s.now
                    b = begin("pT")
                    act.wait_ge(sem["pe_stage"], s.stages())
                    act.activation(big_hi[:, 4096:5120], b[:, 0:2, :].rearrange("p a b -> p (a b)"), ACT.Copy).then_inc(sem["pT_hi"], 1)
                    if h < 3:
                        act.drain()
                        exponentials(scores, scores_step)
                    begin("pv")
                act.wait_ge(sem["o_sq"], s.next("o_sq"))
                act.activation(st[:, 120:128], st[:, 112:120], ACT.Sqrt).then_inc(sem["o_rt"], 1)
                begin("oT")
                act.wait_ge(psum_free[s.now % 2], s.reads())
                o = hf * 1024
                act.activation(big_hi[:, o:o + 1024], at(2048, 1024), ACT.Copy).then_inc(sem["oT_hi"], 1)
            gates1()
            out_strips(2)
            modulated(1, 3, 4, 2)
            ffn(22, 4, 256)
            gates1()
            out_strips(2)

            def turn_x():
                b = begin("xT")
                act.wait_ge(sem["pe_stage"], s.stages())
                act.activation(hT_hi[:, :, 0:256], b.rearrange("p b (c n) -> p (b c) n", c=2), ACT.Copy).then_inc(sem["xT_hi"], 1)

            def ln():
                act.wait_ge(sem["ln_var"], s.next("ln_var"))
                act.activation(st[:, 8:10], st[:, 4:6], ACT.Sqrt).then_inc(sem["ln_rstd"], 1)

            def layer(lay):
                turn_x()
                def strip():
                    b = begin("in")
                    act.wait_ge(sem["unit_used"], s.units())
                    act.activation(NAT, b[:, 0:2, :], ACT.Copy).then_inc(psum_free[s.now % 2], 1)

                def turned(c):
                    b = begin("inT")
                    act.wait_ge(sem["pe_stage"], s.stages())
                    if c == 0:
                        act.activation(QAT.rearrange("p a b -> p (a b)"), b[:, 0:2, :].rearrange("p a b -> p (a b)"), ACT.Copy).then_inc(psum_free[s.now % 2], 1)
                    elif c == 1:
                        act.activation(KAT.rearrange("p a b -> p (a b)"), b[:, 0, :], ACT.Copy)
                        act.activation(QBT[:, 0:2, :].rearrange("p a b -> p (a b)"), b[:, 1, :], ACT.Copy).then_inc(psum_free[s.now % 2], 1)
                    elif c < 4:
                        dst = QBT[:, 2:6, :] if c == 2 else KBT[:, 0:4, :]
                        act.activation(dst.rearrange("p a b -> p (a b)"), b[:, 0:2, :].rearrange("p a b -> p (a b)"), ACT.Copy).then_inc(psum_free[s.now % 2], 1)
                    else:
                        act.activation(KBT[:, 4:6, :].rearrange("p a b -> p (a b)"), b[:, 0, :], ACT.Copy)
                        act.activation(big_hi[:, PIN0:PIN0 + 512], b[:, 1, :], ACT.Copy).then_inc(sem["ple_hi"], 1)

                for c in range(2):
                    strip()
                    turned(c)
                for g in range(2):
                    begin("s")
                    act.wait_ge(sem["max_ready"], s.next("max_ready"))
                    for m in range(8):
                        act.activation(PA.rearrange("p a (b n) -> p (a b) n", b=2)[:, m, :], PA.rearrange("p a (b n) -> p (a b) n", b=2)[:, m, :],
                                       ACT.Exp, scale=0.125, bias=st[:, 100 + m:101 + m], accum_out=st[:, 108 + m:109 + m])
                    act.activation(st[:, 124:132], st[:, 116:124], ACT.Exp).then_inc(sem["p_exp"], 1)
                    strip()
                    b = begin("pT")
                    act.wait_ge(sem["pe_stage"], s.stages())
                    act.activation(big_hi[:, PT0:PT0 + 2048], b.rearrange("p a b -> p (a b)"), ACT.Copy).then_inc(sem["pT_hi"], 1)
                    b = begin("pv")
                    act.wait_ge(sem["pe_stage"], s.stages())
                    for o in range(2):
                        i = act.activation(big(big_hi, OT0 + g * 512, 2, 256)[64 * o:64 * o + 64],
                                           b.rearrange("p (c o) n -> p c o n", o=2)[64 * o:64 * o + 64, :, o, 0:256], ACT.Copy)
                    i.then_inc(sem["oT_hi"], 1)
                    if g == 1:
                        turned(2)
                for c in (3, 4):
                    strip()
                    turned(c)

                def exponentials(sl):
                    act.wait_ge(sem["max_ready"], s.next("max_ready"))
                    pb = PB[sl % 2].rearrange("p g (q n) -> p g q n", q=2)
                    for q in range(2):
                        e = act.activation(pb[:, :, q, :], pb[:, :, q, :], ACT.Exp, scale=0.125,
                                           bias=st[:, 100 + q:101 + q], accum_out=st[:, 104 + q:105 + q])
                    e.then_inc(sem["p_exp"], 1)

                begin("s")
                exponentials(0)
                for sl in range(4):
                    if sl < 3:
                        begin("s")
                    b = begin("pT")
                    act.wait_ge(sem["pe_stage"], s.stages())
                    act.activation(big(big_hi, PT0, 3, 512), b[:, 0:3, :], ACT.Copy).then_inc(sem["pT_hi"], 1)
                    if sl < 3:
                        exponentials(sl + 1)
                    b = begin("pv")
                    act.wait_ge(sem["pe_stage"], s.stages())
                    o = sl % 2
                    act.activation(big_hi[64 * o:64 * o + 64, OT0 + 1024 + (sl // 2) * 256:OT0 + 1280 + (sl // 2) * 256],
                                   b[64 * o:64 * o + 64, 0, 0:256], ACT.Copy).then_inc(sem["oT_hi"], 1)
                for g in range(2):
                    b = begin("gates").rearrange("p b (c n) -> p (b c) n", c=2)
                    act.wait_ge(sem["unit_used"], s.units())
                    for c in range(8):
                        j = g * 8 + c
                        i2 = act.activation(GS[:, j, :], b[:, c, :], ACT.Sigmoid, bias=cols[:, V_BG + lay * 16 + j:V_BG + lay * 16 + j + 1])
                    i2.then_inc(psum_free[s.now % 2], 1)
                begin("branch a")
                begin("branch b")
                act.wait_ge(sem["mix_ready"], s.next("mix_ready"))
                act.activation(big_hi[:, 0:2048], MIX.rearrange("p a b -> p (a b)"), ACT.Copy).then_inc(sem["mix_hi"], 1)
                out_strips(2)
                ln()
                turn_x()
                for c in range(2):
                    begin("ple gate")
                act.wait_ge(sem["gl_ready"], s.next("gl_ready"))
                act.activation(PLE.rearrange("p a b -> p (a b)"), PLE.rearrange("p a b -> p (a b)"), ACT.Sigmoid).then_inc(sem["gs_ready"], 1)
                begin("ple")
                for g in range(4):
                    b = begin("up")
                    act.wait_ge(sem["unit_used"], s.units())
                    if s.count("hid_lo"):
                        act.wait_ge(sem["hid_lo"], s.count("hid_lo"))
                    s.next("hid_lo")
                    act.activation(HID, b.rearrange("p a b -> p (a b)"), ACT.Relu).then_inc(psum_free[s.now % 2], 1)
                    act.wait_ge(sem["sqr_ready"], s.next("sqr_ready"))
                    act.activation(big_hi[:, g * 2048:(g + 1) * 2048], HID, ACT.Copy).then_inc(sem["hid_hi"], 1)
                for _ in range(2):
                    begin("down")
                ln()

            for i in range(2):
                layer(i)

        @block.vector
        def _(dve):
            s = Side()
            drain = dve.drain
            op = dve.tensor_tensor
            ts = dve.tensor_scalar

            def flat(v):
                return v.rearrange("p a b -> p (a b)")

            def split(n):
                while s.split < min(n, TOTAL_UNITS):
                    u = s.split
                    m = SIZES[u]
                    dve.wait_ge(sem["hi_ready"], u + 1 - MOD_UNITS)
                    op(w_lo[:, u % SPLIT_SLOTS, 0:m], raw[:, u % RAW_SLOTS, 0:m],
                       w_hi[:, u % SPLIT_SLOTS, 0:m].bitcast(F32), ALU.subtract).then_inc(sem["lo_ready"], 1)
                    s.split += 1

            def begin(name):
                s.begin(name)
                split(UNITS_BEFORE[s.now + 1] + SPLIT_SLOTS)
                dve.drain()
                return half(s.now)

            def lo(dst, src, hi):
                return op(dst, src, hi.bitcast(F32), ALU.subtract)

            dve.wait_ge(sem["dec_in"], s.next("dec_in", 16))
            x, y, z, w2 = (dec[:, n, :] for n in (0, 2, 3, 4))
            dve.scalar_tensor_tensor(out=dec[:, 1, :], in0=x, scalar=-1.0, in1=x, op0=ALU.mult, op1=ALU.max).then_inc(sem["dec_abs"], 1)
            dve.wait_ge(sem["dec_exp"], s.next("dec_exp"))
            ts(z, y, 2.0, None, ALU.add)
            drain()
            dve.reciprocal(w2, z)
            drain()
            op(z, y, w2, ALU.mult)
            drain()
            op(w2, z, z, ALU.mult)
            drain()
            acc = dec[:, 1, :]
            ts(acc, w2, 1 / 17, None, ALU.mult)
            for n in (15, 13, 11, 9, 7, 5, 3):
                drain()
                dve.scalar_tensor_tensor(out=acc, in0=acc, scalar=1 / n, in1=w2, op0=ALU.add, op1=ALU.mult)
            drain()
            dve.scalar_tensor_tensor(out=acc, in0=acc, scalar=1.0, in1=z, op0=ALU.add, op1=ALU.mult)
            drain()
            ts(acc, acc, 2.0, None, ALU.mult)
            drain()
            dve.scalar_tensor_tensor(out=x, in0=x, scalar=0.0, in1=acc, op0=ALU.min, op1=ALU.subtract)
            drain()
            ts(dec[:, 1, :], x, -1.0, None, ALU.mult)
            ts(dec[:, 2, :], x, 256.0, None, ALU.mult).then_inc(sem["dec_ready"], 1)
            dve.wait_ge(sem["lam_in"], s.next("lam_in", 16))
            lv = lvec.rearrange("p (a b n) -> p a b n", a=2, b=2)
            op(lprod[:, :, :], lv[:, :, 0, :], lv[:, :, 1, :], ALU.mult)
            drain()
            dve.tensor_reduce(lam[:, 0:2], lprod[:, :, :], AX.X, ALU.add).then_inc(sem["lam_arg"], 1)
            dve.wait_ge(sem["lam_exp"], s.next("lam_exp"))
            dve.scalar_tensor_tensor(out=lam[:, 0:1], in0=lam[:, 3:4], scalar=-LAMBDA_INIT, in1=lam[:, 2:3], op0=ALU.add, op1=ALU.subtract)

            b = begin("cols")
            dve.wait_ge(sem["pe_stage"], s.stages())
            dve.tensor_copy(cols[:, 0:161], b[:, 0, 0:161]).then_inc(psum_free[s.now % 2], 1)
            for g in range(6):
                begin("mod rows")
                b = begin("mod cols")
                dve.wait_ge(sem["pe_stage"], s.stages())
                d, c = divmod(g, 3)
                m = mod[:, d, 16 * c:16 * c + 16, :].rearrange("p c s -> p (c s)")
                if c == 0:
                    dve.tensor_copy(m[:, 0:16], b[:, 0, 0:16])
                    ts(m[:, 16:32], b[:, 0, 16:32], 1.0, None, ALU.add).then_inc(psum_free[s.now % 2], 1)
                elif c == 1:
                    dve.tensor_copy(m, b[:, 0, 0:32]).then_inc(psum_free[s.now % 2], 1)
                else:
                    ts(m[:, 0:16], b[:, 0, 0:16], 1.0, None, ALU.add)
                    dve.tensor_copy(m[:, 16:32], b[:, 0, 16:32]).then_inc(psum_free[s.now % 2], 1)

            def modulated(tb):
                drain()
                dve.wait_ge(sem["sq_ready"], s.next("sq_ready"))
                ts(st[:, 4:4 + tb], st[:, 0:tb], 1.0 / D, EPS, ALU.mult, ALU.add)
                drain()
                dve.reciprocal(st[:, 4:4 + tb], st[:, 4:4 + tb]).then_inc(sem["rv_ready"], 1)
                dve.wait_ge(sem["rs_ready"], s.next("rs_ready"))
                for t in range(tb):
                    i = ts(XN4[:, t, :], X4[:, t, :], st[:, 8 + t:9 + t], None, ALU.mult)
                i.then_inc(sem["xn_ready"], 1)
                per = 16 // tb
                for c0 in range(0, KD, per):
                    begin("xT")
                    dve.wait_ge(psum_free[s.now % 2], s.reads())
                    for c in range(c0, c0 + per):
                        src = XN4[:, 0:tb, c * P:(c + 1) * P]
                        dve.tensor_copy(hT_hi[:, c, 0:tb * P].rearrange("p (t n) -> p t n", t=tb), src)
                    drain()
                    for c in range(c0, c0 + per):
                        src = XN4[:, 0:tb, c * P:(c + 1) * P]
                        i = lo(hT_lo[:, c, 0:tb * P].rearrange("p (t n) -> p t n", t=tb), src,
                               hT_hi[:, c, 0:tb * P].rearrange("p (t n) -> p t n", t=tb))
                    i.then_inc(sem["hT_ready"], 1)

            modulated(4)

            def out_lo(h):
                b = begin("oT")
                dve.wait_ge(sem["pe_stage"], s.stages())
                for c in range(4):
                    i = dve.scalar_tensor_tensor(out=GT[:, c, :], in0=b[:, c, :], scalar=cols[:, V_NG + 4 * h + c:V_NG + 4 * h + c + 1],
                                                 in1=GT[:, c, :], op0=ALU.mult, op1=ALU.mult)
                i.then_inc(psum_free[s.now % 2], 1)
                dve.wait_ge(sem["on_hi"], s.next("on_hi"))
                lo(big_lo[:, h * 2048:(h + 1) * 2048], flat(GT), big_hi[:, h * 2048:(h + 1) * 2048]).then_inc(sem["on_lo"], 1)

            for h in range(RH):
                ts(T1, dist, 0.0, None, ALU.max)
                ts(T2, dist, -1.0, 0.0, ALU.mult, ALU.max).then_inc(sem["mask_arg"], 1)
                begin("qk")
                dve.wait_ge(psum_free[s.now % 2], s.reads())
                rc = const[:, C_RC:C_RC + 512].rearrange("p (t n) -> p t n", t=2)
                rs = const[:, C_RS:C_RS + 512].rearrange("p (t n) -> p t n", t=2)
                for t in range(2):
                    for q in range(2):
                        x = QK[:, t, q * 256:(q + 1) * 256]
                        xv = x.rearrange("p (h r n) -> p h r n", h=2, r=2)
                        tv = ROPE.rearrange("p (h r n) -> p h r n", h=2, r=2)
                        sv = rs[:, t, :].rearrange("p (h r n) -> p h r n", h=2, r=2)
                        for r in range(2):
                            op(tv[:, :, r, :], xv[:, :, 1 - r, :], sv[:, :, r, :], ALU.mult)
                        drain()
                        op(x, x, rc[:, t, :], ALU.mult)
                        drain()
                        i = op(x, x, ROPE, ALU.add)
                        if (t, q) != (1, 1):
                            drain()
                i.then_inc(sem["roped"], 1)
                if h:
                    out_lo(h - 1)
                dve.wait_ge(sem["mask_exp"], s.next("mask_exp"))
                op(G2, G2, G1, ALU.add)
                dve.scalar_tensor_tensor(out=T1, in0=dist, scalar=0.0, in1=T1, op0=ALU.is_ge, op1=ALU.mult)
                dve.scalar_tensor_tensor(out=T2, in0=dist, scalar=0.0, in1=T2, op0=ALU.is_le, op1=ALU.mult)
                drain()
                op(G1, T1, T2, ALU.add)
                drain()
                begin("v")
                begin("qkT")
                b = begin("scores").rearrange("p b (h n) -> p (b h) n", h=2)
                dve.wait_ge(sem["pe_stage"], s.stages())
                for t, g in enumerate((G1[:, 128:384], G1[:, 0:256], G2[:, 128:384], G2[:, 0:256], G1[:, 128:384], G1[:, 0:256])):
                    i = op(PT[:, t, :], b[:, t, :], g, ALU.mult)
                i.then_inc(psum_free[s.now % 2], 1)
                begin("gate")
                b = begin("pv")
                dve.wait_ge(sem["pe_stage"], s.stages())
                for t in range(4):
                    dve.bn_stats(st[:, 132 + 6 * t:138 + 6 * t], b[:, t, :])
                drain()
                for t in range(4):
                    dve.bn_aggr(st[:, 160 + 2 * t:162 + 2 * t], st[:, 132 + 6 * t:138 + 6 * t])
                drain()
                mv = st[:, 160:168].rearrange("p (t n) -> p t n", n=2)
                ts(st[:, 4:8], mv[:, :, 1], EPS, None, ALU.add)
                drain()
                dve.reciprocal(st[:, 4:8], st[:, 4:8]).then_inc(sem["var_ready"], 1)
                dve.wait_ge(sem["rstd_ready"], s.next("rstd_ready"))
                for t in range(4):
                    i = ts(ON[:, t, :], b[:, t, :], mv[:, t, 0:1], st[:, 8 + t:9 + t], ALU.subtract, ALU.mult)
                i.then_inc(psum_free[s.now % 2], 1)
            out_lo(RH - 1)

            def gates(d, which, streams):
                drain()
                for m in range(streams):
                    for c in range(KD):
                        i = ts(DIAG[:, (m * KD + c) * P:(m * KD + c + 1) * P], ident, mod[:, d, which * 8 + c, m:m + 1], None, ALU.mult)
                i.then_inc(sem["diag_ready"], 1)
                begin("row gates")
                dve.wait_ge(psum_free[s.now % 2], s.reads())

            def out_strips(n, tb, last=True, k=0):
                for c in range(n):
                    b = begin("out")
                    dve.wait_ge(sem["unit_used"], s.units())
                    c0 = (c % 2) * 512
                    for t in range(tb):
                        i = op(TMP[:, t, :], b[:, t, :], GATE[:, t // 2, c0:c0 + 512], ALU.mult)
                    i.then_inc(psum_free[s.now % 2], 1)
                    drain()
                    i = op(X4[:, 0:tb, c0:c0 + 512], X4[:, 0:tb, c0:c0 + 512], TMP[:, 0:tb, :], ALU.add)
                    if c < n - 1:
                        drain()
                if last:
                    i.then_inc(sem["x_ready"], 1)
                drain()

            def ffn(chunks, per, T):
                c0 = 0
                while c0 < chunks:
                    n = min(per, chunks - c0)
                    b = begin("ffn")
                    dve.wait_ge(sem["unit_used"], s.units())
                    if T == 512:
                        g = b.rearrange("p (c g) n -> p c g n", g=2)[:, 0:n, 1, :]
                    else:
                        g = b.rearrange("p c (g n) -> p c g n", g=2)[:, 0:n, 1, :]
                    dve.wait_ge(sem["silu_ready"], s.next("silu_ready"))
                    v = SILU[:, 0:n * T]
                    v3 = v.rearrange("p (c n) -> p c n", c=n)
                    op(v3, v3, g, ALU.mult).then_inc(psum_free[s.now % 2], 1)
                    dve.wait_ge(sem["hid_hi"], s.next("hid_hi"))
                    lo(big_lo[:, c0 * T:(c0 + n) * T], v, big_hi[:, c0 * T:(c0 + n) * T]).then_inc(sem["hid_lo"], 1)
                    c0 += n

            gates(0, 2, 2)
            dve.wait_ge(sem["x_in"], s.next("x_in", 64))
            out_strips(4, 4)
            modulated(4)
            ffn(11, 2, 512)
            gates(0, 5, 2)
            out_strips(2, 4, last=False)
            ffn(11, 2, 512)
            out_strips(2, 4)
            modulated(4)

            dve.wait_ge(sem["const2_in"], s.next("const2_in", 48))
            dc, ds = const[:, C2_D:C2_D + 128], const[:, C2_D + 128:C2_D + 256]

            def qk_norm(X, tb, gain):
                G = X.rearrange("p t (g n) -> p (t g) n", n=64)
                for t in range(0, tb, 2):
                    op(SQ.rearrange("p (t n) -> p t n", t=2), X[:, t:t + 2, :], X[:, t:t + 2, :], ALU.mult)
                    drain()
                    dve.tensor_reduce(st[:, 32 + 8 * t:48 + 8 * t], SQ.rearrange("p (g n) -> p g n", n=64), AX.X, ALU.add)
                    drain()
                n = 8 * tb
                ts(st[:, 32:32 + n], st[:, 32:32 + n], 1.0 / 64, EPS, ALU.mult, ALU.add)
                drain()
                dve.reciprocal(st[:, 32:32 + n], st[:, 32:32 + n]).then_inc(sem["qk_sq"], 1)
                dve.wait_ge(sem["qk_rt"], s.next("qk_rt"))
                op(G, G, st[:, 64:64 + n].unsqueeze(2).to_broadcast([P, n, 64]), ALU.mult)
                drain()
                op(G, G, gain.unsqueeze(1).to_broadcast([P, n, 64]), ALU.mult)
                drain()
                for t in range(2):
                    rotate(X[:, t, :], dc[:, 64 * t:64 * t + 64], ds[:, 64 * t:64 * t + 64], 8)

            def rotate(x, c, sn, g):
                tv = SQ[:, 0:64 * g].rearrange("p (g h r n) -> p g h r n", g=g, h=2, r=2)
                xv = x.rearrange("p (g h r n) -> p g h r n", g=g, h=2, r=2)
                sv = sn.rearrange("p (h r n) -> p h r n", h=2, r=2)
                for r in range(2):
                    for a in range(2):
                        op(tv[:, :, a, r, :], xv[:, :, a, 1 - r, :], sv[:, a, r, :].unsqueeze(1).to_broadcast([P, g, 16]), ALU.mult)
                drain()
                x3 = x.rearrange("p (g n) -> p g n", g=g)
                op(x3, x3, c.unsqueeze(1).to_broadcast([P, g, 64]), ALU.mult)
                drain()
                i = op(x, x, SQ[:, 0:64 * g], ALU.add)
                drain()
                return i

            for hf in range(2):
                begin("q")
                dve.wait_ge(psum_free[s.now % 2], s.reads())
                qk_norm(QN, 2, const[:, C2_GAIN:C2_GAIN + 64])
                begin("k")
                dve.wait_ge(psum_free[s.now % 2], s.reads())
                qk_norm(KN, 4, const[:, C2_GAIN + 64:C2_GAIN + 128])
                dve.tensor_copy(lam[:, 1:2], lam[:, 0:1]).then_inc(sem["qk_ready"], 1)
                b = begin("v")
                dve.wait_ge(sem["unit_used"], s.units())
                dve.wait_ge(sem["v_hi"], s.next("v_hi"))
                lo(big(big_lo, 2048, 4, 512), b, big(big_hi, 2048, 4, 512)).then_inc(psum_free[s.now % 2], 1)
                begin("qT")
                begin("kT")

                def maxima():
                    b = begin("s")
                    dve.wait_ge(sem["pe_stage"], s.stages())
                    dve.tensor_reduce(st[:, 96:100], b, AX.X, ALU.max)
                    drain()
                    ts(st[:, 100:104], st[:, 96:100], -DDH ** -0.5, None, ALU.mult).then_inc(sem["max_ready"], 1)
                    return s.now

                def mixture(step):
                    dve.drain()
                    dve.wait_ge(psum_free[step % 2], s.reads(step))
                    dve.reciprocal(st[:, 108:112], st[:, 104:108])
                    drain()
                    for q in range(2):
                        ts(st[:, 109 + 2 * q:110 + 2 * q], st[:, 109 + 2 * q:110 + 2 * q], lam[:, 0:1], None, ALU.mult)
                        ts(DP[:, 2 * q, :], DP[:, 2 * q, :], st[:, 108 + 2 * q:109 + 2 * q], None, ALU.mult)
                    drain()
                    for q in range(2):
                        i = dve.scalar_tensor_tensor(out=DP[:, 2 * q, :], in0=DP[:, 2 * q + 1, :], scalar=st[:, 109 + 2 * q:110 + 2 * q],
                                                     in1=DP[:, 2 * q, :], op0=ALU.mult, op1=ALU.add)
                    i.then_inc(sem["p_ready"], 1)

                mixture(maxima())
                for h in range(4):
                    if h < 3:
                        step = maxima()
                    b = begin("pT")
                    dve.wait_ge(sem["pe_stage"], s.stages())
                    dve.wait_ge(sem["pT_hi"], s.next("pT_hi"))
                    lo(big_lo[:, 4096:5120], flat(b[:, 0:2, :]), big_hi[:, 4096:5120]).then_inc(psum_free[s.now % 2], 1)
                    if h < 3:
                        mixture(step)
                    b = begin("pv")
                    dve.wait_ge(sem["pe_stage"], s.stages())
                    dve.tensor_copy(DO[:, :, h * P:(h + 1) * P], b[:, 0, 0:256].rearrange("p (t n) -> p t n", t=2)).then_inc(psum_free[s.now % 2], 1)
                drain()
                sq = at(5120, 8, P)
                og = DO.rearrange("p t (h n) -> p (t h) n", h=4)
                op(sq, og, og, ALU.mult)
                drain()
                dve.tensor_reduce(st[:, 112:120], sq, AX.X, ALU.add)
                drain()
                ts(st[:, 112:120], st[:, 112:120], 1.0 / P, EPS, ALU.mult, ALU.add)
                drain()
                dve.reciprocal(st[:, 112:120], st[:, 112:120]).then_inc(sem["o_sq"], 1)
                dve.wait_ge(sem["o_rt"], s.next("o_rt"))
                op(og, og, st[:, 120:128].unsqueeze(2).to_broadcast([P, 8, P]), ALU.mult).then_inc(sem["o_ready"], 1)
                b = begin("oT")
                dve.wait_ge(sem["pe_stage"], s.stages())
                o = hf * 1024
                ts(at(2048, 1024), flat(b[:, 0:2, :]), cols[:, V_SUB:V_SUB + 1], 1.0 - LAMBDA_INIT, ALU.mult, ALU.mult).then_inc(psum_free[s.now % 2], 1)
                dve.wait_ge(sem["oT_hi"], s.next("oT_hi"))
                lo(big_lo[:, o:o + 1024], at(2048, 1024), big_hi[:, o:o + 1024]).then_inc(sem["oT_lo"], 1)

            gates(1, 2, 1)
            out_strips(2, 2)
            modulated(2)
            ffn(22, 4, 256)
            gates(1, 5, 1)
            out_strips(2, 2, last=False)
            dve.tensor_copy(st[:, 0:1], st[:, 4:5]).then_inc(sem["x_next"], 1)

            def turn_x():
                b = begin("xT").rearrange("p b (c n) -> p (b c) n", c=2)
                dve.wait_ge(sem["pe_stage"], s.stages())
                dve.wait_ge(sem["xT_hi"], s.next("xT_hi"))
                lo(hT_lo[:, :, 0:256], b, hT_hi[:, :, 0:256]).then_inc(psum_free[s.now % 2], 1)

            def ln(loaded, value):
                drain()
                for t in range(2):
                    for c in range(2):
                        dve.bn_stats(st[:, 132 + 12 * t + 6 * c:138 + 12 * t + 6 * c], X2[:, t, c * 512:(c + 1) * 512])
                drain()
                for t in range(2):
                    dve.bn_aggr(st[:, 160 + 2 * t:162 + 2 * t], st[:, 132 + 12 * t:144 + 12 * t])
                drain()
                mv = st[:, 160:164].rearrange("p (t n) -> p t n", n=2)
                ts(st[:, 4:6], mv[:, :, 1], LN_EPS, None, ALU.add)
                drain()
                dve.reciprocal(st[:, 4:6], st[:, 4:6]).then_inc(sem["ln_var"], 1)
                dve.wait_ge(sem["ln_rstd"], s.next("ln_rstd"))
                for t in range(2):
                    ts(X2[:, t, :], X2[:, t, :], mv[:, t, 0:1], st[:, 8 + t:9 + t], ALU.subtract, ALU.mult)
                drain()
                dve.wait_ge(loaded, value)
                for t in range(2):
                    op(X2[:, t, :], X2[:, t, :], LN1G, ALU.mult)
                drain()
                for t in range(2):
                    i = op(X2[:, t, :], X2[:, t, :], LN1B, ALU.add)
                i.then_inc(sem["x_next"], 1)

            bc = const[:, C2_D + 256:C2_D + 288].rearrange("p (t n) -> p t n", t=2)
            bs = const[:, C2_D + 288:C2_D + 320].rearrange("p (t n) -> p t n", t=2)

            def rope16(first, heads):
                tmp = st[:, 32:32 + 0]
                for t in range(2):
                    x = NAT[:, t, 64 * first:64 * (first + heads)].rearrange("p (h n) -> p h n", n=64)
                    tv = KDUP[:, t, 0:16 * heads].rearrange("p (h n) -> p h n", n=16)
                    for r in range(2):
                        op(tv[:, :, 8 * r:8 * r + 8], x[:, :, 8 - 8 * r:16 - 8 * r],
                           bs[:, t, 8 * r:8 * r + 8].unsqueeze(1).to_broadcast([P, heads, 8]), ALU.mult)
                drain()
                for t in range(2):
                    x = NAT[:, t, 64 * first:64 * (first + heads)].rearrange("p (h n) -> p h n", n=64)[:, :, 0:16]
                    op(x, x, bc[:, t, :].unsqueeze(1).to_broadcast([P, heads, 16]), ALU.mult)
                drain()
                for t in range(2):
                    x = NAT[:, t, 64 * first:64 * (first + heads)].rearrange("p (h n) -> p h n", n=64)[:, :, 0:16]
                    tv = KDUP[:, t, 0:16 * heads].rearrange("p (h n) -> p h n", n=16)
                    i = op(x, x, tv, ALU.add)
                drain()
                return i

            VW = 1024
            def vals(x, dst, n):
                hi = big(big_hi, V0, 2, VW)[:, :, dst:dst + n]
                dve.tensor_copy(hi, x)
                drain()
                lo(big(big_lo, V0, 2, VW)[:, :, dst:dst + n], x, hi)

            def layer(i):
                turn_x()
                def strip(c):
                    begin("in")
                    dve.wait_ge(psum_free[s.now % 2], s.reads())
                    if c == 0:
                        rope16(0, 8)
                    elif c == 1:
                        rope16(0, 2)
                        rope16(4, 4)
                        for g in range(2):
                            for r in range(2):
                                dve.tensor_copy(KDUP[:, :, P * g + 64 * r:P * g + 64 * r + 64], NAT[:, :, 64 * g:64 * g + 64])
                                vals(NAT[:, :, 128 + 64 * g:192 + 64 * g], P * g + 64 * r, 64)
                    elif c < 4:
                        rope16(0, 8)
                    elif c == 4:
                        rope16(0, 4)
                        vals(NAT[:, :, 256:512], 256, 256)
                    else:
                        vals(NAT[:, :, 0:512], 512, 512)
                    drain()
                    dve.tensor_copy(st[:, 0:1], lam[:, 0:1]).then_inc(sem["in_ready"], 1)

                def turned(c):
                    if c < 4:
                        begin("inT")
                    elif c == 4:
                        b = begin("inT")
                        dve.wait_ge(sem["pe_stage"], s.stages())
                        dve.wait_ge(sem["ple_hi"], s.next("ple_hi"))
                        lo(big_lo[:, PIN0:PIN0 + 512], b[:, 1, :], big_hi[:, PIN0:PIN0 + 512]).then_inc(psum_free[s.now % 2], 1)

                for c in range(2):
                    strip(c)
                    turned(c)
                dve.wait_ge(sem["mask_in"], s.next("mask_in", 32))
                dve.wait_ge(sem["sink_in"], s.next("sink_in", 16))
                for g in range(2):
                    b = begin("s")
                    dve.wait_ge(sem["pe_stage"], s.stages())
                    op(PA, b, MA.unsqueeze(1).to_broadcast([P, 4, 512]), ALU.add).then_inc(psum_free[s.now % 2], 1)
                    drain()
                    dve.tensor_reduce(st[:, 92:100], PA.rearrange("p a (b n) -> p (a b) n", b=2), AX.X, ALU.max)
                    drain()
                    snk = SINK[:, 4 * g:4 * g + 4].unsqueeze(2).to_broadcast([P, 4, 2])
                    m = st[:, 92:100].rearrange("p (a b) -> p a b", b=2)
                    dve.scalar_tensor_tensor(out=m, in0=m, scalar=0.125, in1=snk, op0=ALU.mult, op1=ALU.max)
                    drain()
                    op(st[:, 116:124].rearrange("p (a b) -> p a b", b=2), snk, m, ALU.subtract)
                    ts(st[:, 100:108], st[:, 92:100], -1.0, None, ALU.mult).then_inc(sem["max_ready"], 1)
                    dve.wait_ge(sem["p_exp"], s.next("p_exp"))
                    op(st[:, 92:100], st[:, 108:116], st[:, 124:132], ALU.add)
                    drain()
                    dve.reciprocal(st[:, 92:100], st[:, 92:100])
                    drain()
                    pa = PA.rearrange("p a (b n) -> p (a b) n", b=2)
                    op(pa, pa, st[:, 92:100].unsqueeze(2).to_broadcast([P, 8, 256]), ALU.mult).then_inc(sem["p_ready"], 1)
                    strip(5 if g == 0 else 2)
                    b = begin("pT")
                    dve.wait_ge(sem["pe_stage"], s.stages())
                    dve.wait_ge(sem["pT_hi"], s.next("pT_hi"))
                    lo(big_lo[:, PT0:PT0 + 2048], flat(b), big_hi[:, PT0:PT0 + 2048]).then_inc(psum_free[s.now % 2], 1)
                    b = begin("pv")
                    dve.wait_ge(sem["pe_stage"], s.stages())
                    dve.wait_ge(sem["oT_hi"], s.next("oT_hi"))
                    for o in range(2):
                        j = lo(big(big_lo, OT0 + g * 512, 2, 256)[64 * o:64 * o + 64],
                               b.rearrange("p (c o) n -> p c o n", o=2)[64 * o:64 * o + 64, :, o, 0:256],
                               big(big_hi, OT0 + g * 512, 2, 256)[64 * o:64 * o + 64])
                    j.then_inc(psum_free[s.now % 2], 1)
                turned(2)
                for c in (3, 4):
                    strip(c)
                    turned(c)

                def maxima(sl):
                    b = begin("s")
                    dve.wait_ge(sem["pe_stage"], s.stages())
                    pb = PB[sl % 2]
                    p4 = pb.rearrange("p g (q n) -> p g q n", q=2)
                    op(pb[:, 0, :], b[:, 0, :], MB[:, 0:512], ALU.add)
                    for g in (1, 2):
                        j = op(p4[:, g, :, :], b[:, g, :].rearrange("p (q n) -> p q n", q=2),
                               MB[:, 256 + 256 * g:512 + 256 * g].unsqueeze(1).to_broadcast([P, 2, 256]), ALU.add)
                    j.then_inc(psum_free[s.now % 2], 1)
                    drain()
                    for q in range(2):
                        dve.tensor_reduce(st[:, 96 + q:97 + q], p4[:, :, q, :], AX.XY, ALU.max)
                    drain()
                    ts(st[:, 100:102], st[:, 96:98], -0.125, None, ALU.mult).then_inc(sem["max_ready"], 1)

                def normalise(sl):
                    p4 = PB[sl % 2].rearrange("p g (q n) -> p g q n", q=2)
                    drain()
                    dve.wait_ge(sem["p_exp"], s.next("p_exp"))
                    dve.reciprocal(st[:, 108:110], st[:, 104:106])
                    drain()
                    for q in range(2):
                        j = ts(p4[:, :, q, :], p4[:, :, q, :], st[:, 108 + q:109 + q], None, ALU.mult)
                    j.then_inc(sem["p_ready"], 1)

                maxima(0)
                normalise(0)
                for sl in range(4):
                    if sl < 3:
                        maxima(sl + 1)
                    b = begin("pT")
                    dve.wait_ge(sem["pe_stage"], s.stages())
                    dve.wait_ge(sem["pT_hi"], s.next("pT_hi"))
                    lo(big(big_lo, PT0, 3, 512), b[:, 0:3, :], big(big_hi, PT0, 3, 512)).then_inc(psum_free[s.now % 2], 1)
                    if sl < 3:
                        normalise(sl + 1)
                    b = begin("pv")
                    dve.wait_ge(sem["pe_stage"], s.stages())
                    dve.wait_ge(sem["oT_hi"], s.next("oT_hi"))
                    o, a = sl % 2, OT0 + 1024 + (sl // 2) * 256
                    lo(big_lo[64 * o:64 * o + 64, a:a + 256], b[64 * o:64 * o + 64, 0, 0:256],
                       big_hi[64 * o:64 * o + 64, a:a + 256]).then_inc(psum_free[s.now % 2], 1)
                for g in range(2):
                    begin("gates")
                b = begin("branch a").rearrange("p b (c n) -> p (b c) n", c=2)
                dve.wait_ge(sem["unit_used"], s.units())
                dve.wait_ge(psum_free[(s.now - 1) % 2], s.reads(s.now - 1))
                op(MIX, b, GS[:, 0:8, :], ALU.mult).then_inc(psum_free[s.now % 2], 1)
                b = begin("branch b").rearrange("p b (c n) -> p (b c) n", c=2)
                dve.wait_ge(sem["unit_used"], s.units())
                op(GS[:, 8:16, :], b, GS[:, 8:16, :], ALU.mult).then_inc(psum_free[s.now % 2], 1)
                drain()
                op(MIX, MIX, GS[:, 8:16, :], ALU.add).then_inc(sem["mix_ready"], 1)
                dve.wait_ge(sem["mix_hi"], s.next("mix_hi"))
                lo(big_lo[:, 0:2048], flat(MIX), big_hi[:, 0:2048]).then_inc(sem["mix_lo"], 1)
                for c in range(2):
                    b = begin("out")
                    dve.wait_ge(sem["unit_used"], s.units())
                    xs = X2[:, :, c * 512:(c + 1) * 512]
                    dve.scalar_tensor_tensor(out=xs, in0=xs, scalar=ALPHA, in1=b[:, 0:2, :], op0=ALU.mult, op1=ALU.add).then_inc(psum_free[s.now % 2], 1)
                drain()
                ln(sem["ln1_in"], s.next("ln1_in", 32))
                turn_x()
                dve.wait_ge(sem["bple_in"], s.next("bple_in", 16))
                for c in range(2):
                    b = begin("ple gate")
                    dve.wait_ge(sem["unit_used"], s.units())
                    j = op(PLE[:, :, c * 512:(c + 1) * 512], b[:, 0:2, :],
                           BPLE[:, c * 512:(c + 1) * 512].unsqueeze(1).to_broadcast([P, 2, 512]), ALU.add)
                    j.then_inc(psum_free[s.now % 2], 1)
                drain()
                dve.tensor_copy(st[:, 0:1], lam[:, 0:1]).then_inc(sem["gl_ready"], 1)
                b = begin("ple").rearrange("p (t c) n -> p t (c n)", t=2)
                dve.wait_ge(sem["unit_used"], s.units())
                dve.wait_ge(sem["gs_ready"], s.next("gs_ready"))
                op(PLE, b, PLE, ALU.mult).then_inc(psum_free[s.now % 2], 1)
                drain()
                dve.scalar_tensor_tensor(out=X2, in0=X2, scalar=ALPHA, in1=PLE, op0=ALU.mult, op1=ALU.add)
                for g in range(4):
                    begin("up")
                    dve.wait_ge(psum_free[s.now % 2], s.reads())
                    op(HID, HID, HID, ALU.mult).then_inc(sem["sqr_ready"], 1)
                    dve.wait_ge(sem["hid_hi"], s.next("hid_hi"))
                    lo(big_lo[:, g * 2048:(g + 1) * 2048], HID, big_hi[:, g * 2048:(g + 1) * 2048]).then_inc(sem["hid_lo"], 1)
                for c in range(2):
                    b = begin("down")
                    dve.wait_ge(sem["unit_used"], s.units())
                    xs = X2[:, :, c * 512:(c + 1) * 512]
                    op(xs, xs, b[:, 0:2, :], ALU.add).then_inc(psum_free[s.now % 2], 1)
                drain()
                ln(sem["ln2_in"], s.next("ln2_in", 32))

            for i in range(2):
                layer(i)

        @block.tensor
        def _(pe):
            s = Side()

            def begin(name):
                s.begin(name)
                return half(s.now)

            def weights(nk):
                u = s.unit
                pe.wait_ge(sem["lo_ready"], u + 1 - MOD_UNITS)
                s.unit += 1
                m = SIZES[u]
                return [w[:, u % SPLIT_SLOTS, 0:m].rearrange("p (k n) -> p k n", k=nk) for w in (w_hi, w_lo)]

            def product(out, a, b, start, stop):
                pe.matmul(out, a[0], b[0], start=start, stop=False)
                pe.matmul(out, a[0], b[1], start=False, stop=False)
                return pe.matmul(out, a[1], b[0], start=False, stop=stop)

            def used(i):
                i.then_inc(sem["unit_used"], 1)

            def staged(i):
                i.then_inc(sem["pe_stage"], 1)

            def rows(out, x, k0, nk, total, tb):
                w = weights(nk)
                for k in range(nk):
                    for t in range(tb):
                        xs = [v[:, t * P:(t + 1) * P] for v in x(k0 + k)]
                        i = product(out(t), xs, [v[:, k, :] for v in w], k0 + k == 0, k0 + k == total - 1)
                used(i)

            def feats(outs, x, T, nk=KD):
                w = weights(nk)
                for j, o in enumerate(outs):
                    for k in range(nk):
                        i = product(o, [v[:, k, j * P:(j + 1) * P] for v in w], [v[:, 0:T] for v in x(k)], k == 0, k == nk - 1)
                used(i)

            def hT(k):
                return hT_hi[:, k, :], hT_lo[:, k, :]

            def bigx(a, T):
                return lambda k: (big_hi[:, a + k * T:a + (k + 1) * T], big_lo[:, a + k * T:a + (k + 1) * T])

            def turn(out, src):
                return pe.transpose(out, src, ident[0:src.shape[0], 0:src.shape[0]])

            pe.wait_ge(sem["const_in"], s.next("const_in", 16))
            pe.wait_ge(sem["vec_in"], s.next("vec_in", 96))
            b = begin("cols")
            turn(b[:, 0, 0:P], vec[:, :])
            staged(turn(b[:, 0, P:P + 33], vec2[0:33, :]))
            pe.wait_ge(sem["silu_c"], s.next("silu_c"))
            for g in range(6):
                b = begin("mod rows")
                if s.now >= 2:
                    pe.wait_ge(psum_free[s.now % 2], s.reads(s.now - 2))
                for j in range(8):
                    w = raw[:, s.unit % RAW_SLOTS, :].rearrange("p (k n) -> p k n", k=4)
                    pe.wait_ge(unit_in[s.unit % RAW_SLOTS], 32 * (s.unit // RAW_SLOTS + 1))
                    s.unit += 1
                    for k in range(4):
                        kk = (j % 2) * 4 + k
                        i = pe.matmul(b[0:2, j // 2, :], st[:, 16 + kk:32:8], w[:, k, :], start=(kk == 0), stop=(kk == 7))
                    used(i)
                b = begin("mod cols")
                pe.wait_ge(psum_free[s.now % 2], s.reads(s.now - 2))
                pe.wait_ge(psum_free[(s.now - 1) % 2], s.reads(s.now - 1))
                pe.wait_ge(sem["bias_in"], s.next("bias_in", 16))
                for j in range(16):
                    i = pe.matmul(b[:, 0, 2 * j:2 * j + 2], MROW[0:3, j * P:(j + 1) * P], select[0:3, :], start=True, stop=True)
                staged(i)

            def modulated(tb):
                pe.wait_ge(sem["xn_ready"], s.next("xn_ready"))
                per = 16 // tb
                for c0 in range(0, KD, per):
                    b = begin("xT").rearrange("p b n -> p (b n)")
                    pe.wait_ge(psum_free[s.now % 2], s.reads(s.now - 2))
                    for c in range(per):
                        for t in range(tb):
                            i = turn(b[:, (c * tb + t) * P:(c * tb + t + 1) * P], XN4[:, t, (c0 + c) * P:(c0 + c + 1) * P])
                    staged(i)
                pe.wait_ge(sem["hT_ready"], s.next("hT_ready", KD // per))

            def gates(streams):
                b = begin("row gates")
                pe.wait_ge(psum_free[s.now % 2], s.reads(s.now - 2))
                pe.wait_ge(sem["diag_ready"], s.next("diag_ready"))
                for n in range(2 * streams):
                    i = pe.matmul(b[:, n, :], ones[:], DIAG[:, n * 512:(n + 1) * 512], start=True, stop=True)
                staged(i)

            def strips(x, total, tb, groups, name="out"):
                b = begin(name)
                pe.wait_ge(psum_free[s.now % 2], s.reads(s.now - 2))
                for k0, nk in groups:
                    rows(lambda t: b[:, t, :], x, k0, nk, total, tb)

            modulated(4)
            pe.wait_ge(sem["ones_set"], s.next("ones_set"))
            def out_turned(last=False):
                b = begin("oT")
                pe.wait_ge(psum_free[s.now % 2], s.reads(s.now - 2))
                if last:
                    pe.wait_ge(psum_free[(s.now - 1) % 2], s.reads(s.now - 1))
                for c in range(4):
                    for t in range(4):
                        i = turn(b[:, c, t * P:(t + 1) * P], ON[:, t, c * P:(c + 1) * P])
                staged(i)

            for h in range(RH):
                b = begin("qk")
                pe.wait_ge(psum_free[s.now % 2], s.reads(s.now - 2))
                for q in range(2):
                    w = weights(KD)
                    for k in range(KD):
                        for t in range(4):
                            xs = [v[:, t * P:(t + 1) * P] for v in hT(k)]
                            i = product(b[:, t, q * 256:(q + 1) * 256], xs, [v[:, k, :] for v in w], k == 0, k == KD - 1)
                    used(i)
                if h:
                    out_turned()
                strips(hT, KD, 4, ((0, 4), (4, 4)), "v")
                b = begin("qkT")
                pe.wait_ge(psum_free[s.now % 2], s.reads(s.now - 2))
                pe.wait_ge(sem["roped"], s.next("roped"))
                for c in range(4):
                    for t in range(4):
                        i = turn(b[:, c, t * P:(t + 1) * P], QK[:, t, c * P:(c + 1) * P])
                staged(i)
                b = begin("scores").rearrange("p b (h n) -> p (b h) n", h=2)
                pe.wait_ge(psum_free[s.now % 2], s.reads(s.now - 2))
                pe.wait_ge(psum_free[(s.now - 1) % 2], s.reads(s.now - 1))
                for t, (j, q0) in enumerate(((0, 0), (1, 0), (2, 0), (3, 0), (2, 256), (3, 256))):
                    for c in range(2):
                        i = pe.matmul(b[:, t, :], QKT[:, 2 + c, j * P:(j + 1) * P], QKT[:, c, q0:q0 + 256], start=(c == 0), stop=(c == 1))
                staged(i)
                b = begin("gate")
                pe.wait_ge(psum_free[s.now % 2], s.reads(s.now - 2))
                for g in range(2):
                    feats([b[:, 2 * g, :], b[:, 2 * g + 1, :]], hT, 512)
                b = begin("pv")
                pe.wait_ge(psum_free[s.now % 2], s.reads(s.now - 2))
                pe.wait_ge(psum_free[(s.now - 2) % 2], s.reads(s.now - 2))
                for t in range(4):
                    keys = [(0, 0), (1, 1), (2, 2), (3, 3)] if t < 2 else [(4, 2), (5, 3)]
                    for n, (m, j) in enumerate(keys):
                        i = pe.matmul(b[:, t, :], PT[:, m, (t % 2) * P:(t % 2 + 1) * P], VN[:, j, :], start=(n == 0), stop=(n == len(keys) - 1))
                staged(i)
            out_turned(last=True)

            gates(2)
            pe.wait_ge(sem["on_lo"], s.next("on_lo", RH))
            for kh in range(2):
                for _ in range(2):
                    strips(bigx(kh * 4096, 512), KD, 4, ((0, 4), (4, 4)))
            modulated(4)

            def ffn_in(chunks, per, T):
                c0 = 0
                while c0 < chunks:
                    n = min(per, chunks - c0)
                    b = begin("ffn")
                    pe.wait_ge(psum_free[s.now % 2], s.reads(s.now - 2))
                    for c in range(n):
                        outs = [b[:, 2 * c, :], b[:, 2 * c + 1, :]] if T == 512 else [b[:, c, 0:256], b[:, c, 256:512]]
                        feats(outs, hT, T)
                    c0 += n

            for hf in range(2):
                ffn_in(11, 2, 512)
                if hf == 0:
                    gates(2)
                pe.wait_ge(sem["hid_lo"], s.next("hid_lo", 6))
                for _ in range(2):
                    strips(bigx(0, 512), 11, 4, ((0, 4), (4, 4), (8, 3)))
            modulated(4)

            for hf in range(2):
                strips(hT, KD, 2, ((0, 4), (4, 4)), "q")
                strips(hT, KD, 4, ((0, 4), (4, 4)), "k")
                strips(hT, KD, 4, ((0, 4), (4, 4)), "v")
                b = begin("qT")
                pe.wait_ge(psum_free[s.now % 2], s.reads(s.now - 2))
                pe.wait_ge(sem["qk_ready"], s.next("qk_ready"))
                for c in range(4):
                    for t in range(2):
                        i = turn(b[:, c // 2, (c % 2) * 256 + t * P:(c % 2) * 256 + (t + 1) * P], QN[:, t, c * P:(c + 1) * P])
                staged(i)
                b = begin("kT")
                pe.wait_ge(psum_free[s.now % 2], s.reads(s.now - 2))
                for c in range(4):
                    for t in range(4):
                        i = turn(b[:, c, t * P:(t + 1) * P], KN[:, t, c * P:(c + 1) * P])
                staged(i)
                pe.wait_ge(psum_free[(s.now) % 2], s.reads(s.now))

                def scores(h):
                    b = begin("s")
                    pe.wait_ge(psum_free[s.now % 2], s.reads(s.now - 2))
                    for q in range(2):
                        for m in range(2):
                            r = slice(64 * m, 64 * m + 64)
                            i = pe.matmul(b[:, 2 * q + m, :], DQT[r, h, q * P:(q + 1) * P], DKT[r, h, :], start=True, stop=True)
                    staged(i)

                def turned(h):
                    b = begin("pT")
                    pe.wait_ge(psum_free[s.now % 2], s.reads(s.now - 2))
                    pe.wait_ge(sem["p_ready"], s.next("p_ready"))
                    for q in range(2):
                        for j in range(4):
                            i = turn(b[:, q, j * P:(j + 1) * P], DP[:, 2 * q, j * P:(j + 1) * P])
                    staged(i)
                    b = begin("pv")
                    pe.wait_ge(psum_free[s.now % 2], s.reads(s.now - 2))
                    pe.wait_ge(psum_free[(s.now - 1) % 2], s.reads(s.now - 1))
                    for q in range(2):
                        for j in range(4):
                            pt = [v[:, 4096 + (4 * q + j) * P:4096 + (4 * q + j + 1) * P] for v in (big_hi, big_lo)]
                            vv = [big(v, 2048, 4, 512)[:, j, h * P:(h + 1) * P] for v in (big_hi, big_lo)]
                            i = product(b[:, 0, q * P:(q + 1) * P], pt, vv, j == 0, j == 3)
                    staged(i)

                scores(0)
                for h in range(1, 4):
                    scores(h)
                    turned(h - 1)
                turned(3)
                b = begin("oT")
                pe.wait_ge(psum_free[s.now % 2], s.reads(s.now - 2))
                pe.wait_ge(sem["o_ready"], s.next("o_ready"))
                for c in range(4):
                    for t in range(2):
                        i = turn(b[:, c // 2, (c % 2) * 256 + t * P:(c % 2) * 256 + (t + 1) * P], DO[:, t, c * P:(c + 1) * P])
                staged(i)
            gates(1)
            pe.wait_ge(sem["oT_lo"], s.next("oT_lo", 2))
            for _ in range(2):
                strips(bigx(0, 256), KD, 2, ((0, 4), (4, 4)))
            modulated(2)
            ffn_in(22, 4, 256)
            gates(1)
            pe.wait_ge(sem["hid_lo"], s.next("hid_lo", 6))
            for _ in range(2):
                strips(bigx(0, 256), 22, 2, [(k, min(4, 22 - k)) for k in range(0, 22, 4)])

            def turn_x():
                pe.wait_ge(sem["x_next"], s.next("x_next"))
                b = begin("xT").rearrange("p b (c n) -> p (b c) n", c=2)
                pe.wait_ge(psum_free[s.now % 2], s.reads(s.now - 2))
                for c in range(KD):
                    for t in range(2):
                        i = turn(b[:, c, t * P:(t + 1) * P], X2[:, t, c * P:(c + 1) * P])
                staged(i)
                pe.wait_ge(psum_free[(s.now) % 2], s.reads(s.now))

            def layer():
                turn_x()
                def turned(c):
                    pe.wait_ge(sem["in_ready"], s.next("in_ready"))
                    b = begin("inT").rearrange("p b (c n) -> p (b c) n", c=2)
                    pe.wait_ge(psum_free[s.now % 2], s.reads(s.now - 2))
                    if c == 1:
                        where = [(KDUP, 0), (KDUP, 1), (NAT, 2), (NAT, 3)]
                    elif c == 4:
                        pe.wait_ge(sem["p_in"], s.next("p_in", 16))
                        where = [(NAT, 0), (NAT, 1), (PIN, 0), (PIN, 1)]
                    else:
                        where = [(NAT, j) for j in range(4)]
                    for j, (v, f) in enumerate(where):
                        for t in range(2):
                            i = turn(b[:, j, t * P:(t + 1) * P], v[:, t, f * P:(f + 1) * P])
                    staged(i)

                for c in range(2):
                    strips(hT, KD, 2, ((0, 4), (4, 4)), "in")
                    turned(c)
                pe.wait_ge(psum_free[(s.now) % 2], s.reads(s.now))
                for g in range(2):
                    b = begin("s")
                    pe.wait_ge(psum_free[s.now % 2], s.reads(s.now - 2))
                    for h in range(4):
                        f, r = 2 * g + h // 2, slice(64 * (h % 2), 64 * (h % 2) + 64)
                        for q in range(2):
                            i = pe.matmul(b[:, h, q * 256:(q + 1) * 256], QAT[r, f, q * P:(q + 1) * P], KAT[r, g, :], start=True, stop=True)
                    staged(i)
                    if g == 1:
                        pe.wait_ge(sem["in_ready"], s.next("in_ready"))
                    strips(hT, KD, 2, ((0, 4), (4, 4)), "in")
                    b = begin("pT")
                    pe.wait_ge(psum_free[s.now % 2], s.reads(s.now - 2))
                    pe.wait_ge(sem["p_ready"], s.next("p_ready"))
                    for h in range(4):
                        for q in range(2):
                            for j in range(2):
                                i = turn(b[:, h, j * 256 + q * P:j * 256 + (q + 1) * P], PA[:, h, q * 256 + j * P:q * 256 + (j + 1) * P])
                    staged(i)
                    b = begin("pv")
                    pe.wait_ge(psum_free[s.now % 2], s.reads(s.now - 2))
                    pe.wait_ge(psum_free[(s.now - 1) % 2], s.reads(s.now - 1))
                    for h in range(4):
                        for j in range(2):
                            vv = [big(v, V0, 2, 1024)[:, j, g * P:(g + 1) * P] for v in (big_hi, big_lo)]
                            a = PT0 + (2 * h + j) * 256
                            i = product(b[:, h, 0:256], vv, [v[:, a:a + 256] for v in (big_hi, big_lo)], j == 0, j == 1)
                    staged(i)
                turned(2)
                for c in (3, 4):
                    strips(hT, KD, 2, ((0, 4), (4, 4)), "in")
                    turned(c)

                def scores(sl):
                    b = begin("s")
                    pe.wait_ge(psum_free[s.now % 2], s.reads(s.now - 2))
                    if sl == 0:
                        pe.wait_ge(psum_free[(s.now - 1) % 2], s.reads(s.now - 1))
                    r = slice(64 * (sl % 2), 64 * (sl % 2) + 64)
                    for g in range(3):
                        f = 2 * g + sl // 2
                        for q in range(2):
                            i = pe.matmul(b[:, g, q * 256:(q + 1) * 256], QBT[r, f, q * P:(q + 1) * P], KBT[r, f, :], start=True, stop=True)
                    staged(i)

                scores(0)
                for sl in range(4):
                    if sl < 3:
                        scores(sl + 1)
                    b = begin("pT")
                    pe.wait_ge(psum_free[s.now % 2], s.reads(s.now - 2))
                    pe.wait_ge(sem["p_ready"], s.next("p_ready"))
                    for g in range(3):
                        for q in range(2):
                            for j in range(2):
                                i = turn(b[:, g, j * 256 + q * P:j * 256 + (q + 1) * P], PB[sl % 2][:, g, q * 256 + j * P:q * 256 + (j + 1) * P])
                    staged(i)
                    b = begin("pv")
                    pe.wait_ge(psum_free[s.now % 2], s.reads(s.now - 2))
                    pe.wait_ge(psum_free[(s.now - 1) % 2], s.reads(s.now - 1))
                    for g in range(3):
                        for j in range(2):
                            f = 256 + (g * 4 + (sl // 2) * 2) * 64
                            vv = [big(v, V0, 2, 1024)[:, j, f:f + P] for v in (big_hi, big_lo)]
                            a = PT0 + (2 * g + j) * 256
                            i = product(b[:, 0, 0:256], vv, [v[:, a:a + 256] for v in (big_hi, big_lo)], g == j == 0, g == 2 and j == 1)
                    staged(i)
                for g in range(2):
                    b = begin("gates").rearrange("p b (c n) -> p (b c) n", c=2)
                    pe.wait_ge(psum_free[s.now % 2], s.reads(s.now - 2))
                    for n in range(4):
                        feats([b[:, 2 * n, :], b[:, 2 * n + 1, :]], hT, 256)
                b = begin("branch a").rearrange("p b (c n) -> p (b c) n", c=2)
                pe.wait_ge(psum_free[s.now % 2], s.reads(s.now - 2))
                for n in range(2):
                    feats([b[:, 4 * n + j, :] for j in range(4)], bigx(OT0, 256), 256, nk=4)
                b = begin("branch b").rearrange("p b (c n) -> p (b c) n", c=2)
                pe.wait_ge(psum_free[s.now % 2], s.reads(s.now - 2))
                feats([b[:, j, :] for j in range(8)], bigx(OT0 + 1024, 256), 256, nk=2)
                pe.wait_ge(sem["mix_lo"], s.next("mix_lo"))
                for _ in range(2):
                    strips(bigx(0, 256), KD, 2, ((0, 4), (4, 4)))
                turn_x()
                for _ in range(2):
                    strips(hT, KD, 2, ((0, 4), (4, 4)), "ple gate")
                b = begin("ple")
                pe.wait_ge(psum_free[s.now % 2], s.reads(s.now - 2))
                w = weights(2)
                for t in range(2):
                    for c in range(2):
                        for k in range(2):
                            xs = [v[:, PIN0 + k * 256 + t * P:PIN0 + k * 256 + (t + 1) * P] for v in (big_hi, big_lo)]
                            i = product(b[:, 2 * t + c, :], xs, [v[:, k, c * 512:(c + 1) * 512] for v in w], k == 0, k == 1)
                used(i)
                for g in range(4):
                    b = begin("up").rearrange("p b (c n) -> p (b c) n", c=2)
                    pe.wait_ge(psum_free[s.now % 2], s.reads(s.now - 2))
                    for n in range(4):
                        feats([b[:, 2 * n, :], b[:, 2 * n + 1, :]], hT, 256)
                pe.wait_ge(sem["hid_lo"], s.next("hid_lo", 4))
                for _ in range(2):
                    strips(bigx(0, 256), 32, 2, [(k, 4) for k in range(0, 32, 4)], "down")

            for _ in range(2):
                layer()
            assert s.step == len(PLAN) and s.unit == TOTAL_UNITS


def table():
    import numpy as np
    f = np.float32
    t = np.zeros((P, C_ALL), f)
    p = np.arange(P)
    t[:, C_IDENT:C_IDENT + P] = np.eye(P, dtype=f)
    t[:, C_DIST:C_DIST + 384] = np.arange(384)[None, :] - P - p[:, None]
    t[:, C_SEL:C_SEL + 2] = [[r == c or r == 2 for c in range(2)] for r in range(P)]

    def rotation(pos, base, n, step):
        inv = np.power(f(base), (-np.arange(n, dtype=f) * f(step) / f(n * step))).astype(f)
        a = (pos.astype(f)[:, None] * inv[None, :]).astype(f)
        return np.cos(a).astype(f), np.sin(a).astype(f)

    for a, quarter, c0, s0, width in ((0, 64, C_RC, C_RS, 256), (0, 16, C_DC, C_DS, 64)):
        for tb in range(2):
            pos = tb * P + p
            parts = [rotation(q, 10000.0, quarter, 1) for q in (pos // 64, pos % 64)]
            t[:, c0 + tb * width:c0 + (tb + 1) * width] = np.concatenate([v for c, s in parts for v in (c, c)], 1)
            t[:, s0 + tb * width:s0 + (tb + 1) * width] = np.concatenate([v for c, s in parts for v in (-s, s)], 1)
    for tb in range(2):
        c, s = rotation(tb * P + p, 500000.0, 8, 2)
        t[:, C_BC + tb * 16:C_BC + tb * 16 + 16] = np.concatenate([c, c], 1)
        t[:, C_BS + tb * 16:C_BS + tb * 16 + 16] = np.concatenate([-s, s], 1)
    j = np.arange(256)[None, :]
    for tb in range(2):
        d = np.abs(tb * P + p[:, None] - j)
        t[:, C_MA + tb * 256:C_MA + (tb + 1) * 256] = np.where(d <= 128, 0, MASKED)
        t[:, C_MB + tb * 256:C_MB + (tb + 1) * 256] = np.where(d <= 64, 0, MASKED)
    for n, r in enumerate((4, 16)):
        t[:, C_MB + 512 + n * 256:C_MB + 768 + n * 256] = np.where((p[:, None] - j) % r == 0, 0, MASKED)
    return t


NAMES = ["x", "c", "ctx", "c_ctx", "ada_w", "ada_b", "ret_w_in", "ret_decay_logit", "ret_norm_g", "ret_w_out",
         "diff_w_in", "diff_q_norm_g", "diff_k_norm_g", "diff_lambda", "diff_subln_g", "diff_w_out",
         "ffn_w_in", "ffn_w_out", "p_2", "w_in_2", "b_gate_2", "a_sink_2", "w_branch_a_2", "w_branch_b_2",
         "w_out_2", "ln1_g_2", "ln1_b_2", "w_up_2", "w_down_2", "w_ple_gate_2", "b_ple_gate_2", "w_ple_2",
         "ln2_g_2", "ln2_b_2"]


def kernel(**inputs):
    import numpy as np
    import concourse.bacc as bacc
    from concourse.bass_utils import run_bass_kernel_spmd

    nc = bacc.Bacc("TRN2", target_bir_lowering=False, num_devices=1)
    arrays = {name: np.ascontiguousarray(inputs[name]) for name in NAMES}
    arrays["table"] = table()
    A = {n: nc.dram_tensor(n, a.shape, mybir.dt.from_np(a.dtype), kind="ExternalInput").ap() for n, a in arrays.items()}
    out = nc.dram_tensor("out", (1, SEQ, D), F32, kind="ExternalOutput").ap()
    build(nc, A, out)
    return run_bass_kernel_spmd(nc, [arrays], core_ids=[0]).results[0]["out"]
```
